# Optimizing a Trainium2 kernel written in Bass

```python
import math
import jax, jax.numpy as jnp
from jax import lax
import numpy as np

D_MODEL = 2048
BATCH = 1
SEQ = 512
DEPTH = 1

D_MIX = D_MODEL
SSM_WIDTH = D_MIX // 2
SSM_GROUP = 16
SSM_GROUPS = SSM_WIDTH // SSM_GROUP
SSM_STATE = 64
SSM_CHUNK = 128
DIFF_WIDTH = D_MIX // 4
DIFF_HEADS = 4
DIFF_HEAD_DIM = DIFF_WIDTH // (2 * DIFF_HEADS)
DIFF_V_DIM = 2 * DIFF_HEAD_DIM
XATTN_WIDTH = D_MIX - SSM_WIDTH - DIFF_WIDTH
XATTN_HEADS = 4
XATTN_HEAD_DIM = XATTN_WIDTH // XATTN_HEADS
MEM_TOKENS = 256
ROPE_THETA = 10000.0
Q_BLOCK = 128
NORM_EPS = 1e-6
MASK_VALUE = -1e30


def rmsnorm(x, g):
    x32 = x.astype(jnp.float32)
    var = jnp.mean(x32 * x32, axis=-1, keepdims=True)
    return (x32 * lax.rsqrt(var + NORM_EPS) * g.astype(jnp.float32)).astype(x.dtype)

def rope_tables(positions, dim):
    inv = ROPE_THETA ** (-jnp.arange(0, dim, 2, dtype=jnp.float32) / dim)
    ang = positions.astype(jnp.float32)[..., None] * inv
    return jnp.cos(ang), jnp.sin(ang)

def apply_rope(x, cos, sin):
    extra = x.ndim - 3
    shp = cos.shape[:2] + (1,) * extra + cos.shape[-1:]
    c, s = cos.reshape(shp), sin.reshape(shp)
    x1, x2 = jnp.split(x.astype(jnp.float32), 2, axis=-1)
    return jnp.concatenate([x1 * c - x2 * s, x2 * c + x1 * s], axis=-1).astype(x.dtype)

def s5_scan(u, a_re, a_im, log_dt, b_re, b_im, c_re, c_im, d_skip):
    f32 = jnp.float32
    bsz, seq = u.shape[0], u.shape[1]
    n_chunks = seq // SSM_CHUNK
    dt = jnp.exp(log_dt.astype(f32))[:, None]
    lr, li = a_re.astype(f32), a_im.astype(f32)
    mag = jnp.exp(lr * dt)
    abar_re, abar_im = mag * jnp.cos(li * dt), mag * jnp.sin(li * dt)
    den = lr * lr + li * li
    nr, ni = abar_re - 1.0, abar_im
    z_re = (nr * lr + ni * li) / den
    z_im = (ni * lr - nr * li) / den
    br, bi = b_re.astype(f32), b_im.astype(f32)
    bbar_re = z_re[..., None] * br - z_im[..., None] * bi
    bbar_im = z_re[..., None] * bi + z_im[..., None] * br
    cr, ci = c_re.astype(f32), c_im.astype(f32)

    uc = u.astype(f32).reshape(bsz, n_chunks, SSM_CHUNK, SSM_GROUPS, SSM_GROUP)
    uc = uc.transpose(1, 2, 0, 3, 4)
    a_el_re = jnp.broadcast_to(abar_re[None, None], (SSM_CHUNK, 1, SSM_GROUPS, SSM_STATE))
    a_el_im = jnp.broadcast_to(abar_im[None, None], (SSM_CHUNK, 1, SSM_GROUPS, SSM_STATE))

    def combine(e1, e2):
        a1r, a1i, b1r, b1i = e1
        a2r, a2i, b2r, b2i = e2
        return (a2r * a1r - a2i * a1i,
                a2r * a1i + a2i * a1r,
                a2r * b1r - a2i * b1i + b2r,
                a2r * b1i + a2i * b1r + b2i)

    def chunk_step(carry, u_t):
        h_re, h_im = carry
        bu_re = jnp.einsum('tbgh,gph->tbgp', u_t, bbar_re)
        bu_im = jnp.einsum('tbgh,gph->tbgp', u_t, bbar_im)
        pa_re, pa_im, s_re, s_im = lax.associative_scan(
            combine, (a_el_re, a_el_im, bu_re, bu_im), axis=0)
        x_re = s_re + pa_re * h_re - pa_im * h_im
        x_im = s_im + pa_re * h_im + pa_im * h_re
        y = jnp.einsum('tbgp,ghp->tbgh', x_re, cr) - jnp.einsum('tbgp,ghp->tbgh', x_im, ci)
        return (x_re[-1], x_im[-1]), y

    h0 = (jnp.zeros((bsz, SSM_GROUPS, SSM_STATE), f32), jnp.zeros((bsz, SSM_GROUPS, SSM_STATE), f32))
    _, ys = lax.scan(chunk_step, h0, uc)
    y = ys.transpose(2, 0, 1, 3, 4).reshape(bsz, seq, SSM_WIDTH)
    y = y + d_skip.astype(f32).reshape(SSM_WIDTH) * u.astype(f32)
    return y.astype(u.dtype)

def diff_attention(q, k, v, lam, lambda_init, subln_g):
    bsz, seq = q.shape[0], q.shape[1]
    n_blocks = seq // Q_BLOCK
    scale = DIFF_HEAD_DIM ** -0.5
    k_pos = jnp.arange(seq)
    qb = q.reshape(bsz, n_blocks, Q_BLOCK, DIFF_HEADS, 2, DIFF_HEAD_DIM).transpose(1, 0, 2, 3, 4, 5)

    def block(args):
        qi, blk = args
        s = jnp.einsum('bqhcd,bkhcd->bhcqk', qi, k).astype(jnp.float32) * scale
        q_pos = blk * Q_BLOCK + jnp.arange(Q_BLOCK)
        mask = k_pos[None, :] <= q_pos[:, None]
        s = jnp.where(mask, s, MASK_VALUE)
        p = jax.nn.softmax(s, axis=-1)
        w = p[:, :, 0] - lam * p[:, :, 1]
        return jnp.einsum('bhqk,bkhd->bqhd', w.astype(v.dtype), v)

    o = lax.map(block, (qb, jnp.arange(n_blocks)))
    o = o.transpose(1, 0, 2, 3, 4).reshape(bsz, seq, DIFF_HEADS, DIFF_V_DIM)
    o = rmsnorm(o, subln_g) * (1.0 - lambda_init)
    return o.reshape(bsz, seq, DIFF_WIDTH)

def memory_attention(q, mem_n, w_mem_kv):
    bsz, seq = q.shape[0], q.shape[1]
    kv = mem_n @ w_mem_kv
    mk, mv = jnp.split(kv, 2, axis=-1)
    mk = mk.reshape(bsz, MEM_TOKENS, XATTN_HEADS, XATTN_HEAD_DIM)
    mv = mv.reshape(bsz, MEM_TOKENS, XATTN_HEADS, XATTN_HEAD_DIM)
    s = jnp.einsum('bqhd,bmhd->bhqm', q, mk).astype(jnp.float32) * (XATTN_HEAD_DIM ** -0.5)
    p = jax.nn.softmax(s, axis=-1).astype(mv.dtype)
    o = jnp.einsum('bhqm,bmhd->bqhd', p, mv)
    return o.reshape(bsz, seq, XATTN_WIDTH)

def first_inputs(seed: int = 0) -> dict:
    key = jax.random.key(seed)
    ks = jax.random.split(key, 24)
    f32 = jnp.float32
    in_cols = 2 * SSM_WIDTH + 4 * DIFF_WIDTH + 2 * XATTN_WIDTH
    nrm = lambda k, shp, s: jax.random.normal(k, shp, f32) * s
    x = jax.random.normal(ks[0], (BATCH, SEQ, D_MODEL), f32)
    mem = jax.random.normal(ks[1], (BATCH, MEM_TOKENS, D_MODEL), f32)
    positions = jnp.broadcast_to(jnp.arange(SEQ, dtype=jnp.int32), (BATCH, SEQ))
    norm_pre = 1.0 + nrm(ks[2], (DEPTH, D_MODEL), 0.02)
    norm_post = 1.0 + nrm(ks[3], (DEPTH, D_MODEL), 0.02)
    norm_mem = 1.0 + nrm(ks[4], (DEPTH, D_MODEL), 0.02)
    w_in = nrm(ks[5], (DEPTH, D_MODEL, in_cols), D_MODEL ** -0.5)
    w_out = nrm(ks[6], (DEPTH, D_MIX, D_MODEL), D_MIX ** -0.5)
    w_mem_kv = nrm(ks[7], (DEPTH, D_MODEL, 2 * XATTN_WIDTH), D_MODEL ** -0.5)
    gp = (DEPTH, SSM_GROUPS, SSM_STATE)
    ssm_a_re = -0.5 + nrm(ks[8], gp, 0.01)
    ssm_a_im = jnp.pi * jnp.arange(SSM_STATE, dtype=f32)[None, None, :] + nrm(ks[9], gp, 0.01)
    ssm_log_dt = jax.random.uniform(ks[10], (DEPTH, SSM_GROUPS), f32, math.log(1e-3), math.log(1e-1))
    ssm_b_re = nrm(ks[11], (DEPTH, SSM_GROUPS, SSM_STATE, SSM_GROUP), (2 * SSM_GROUP) ** -0.5)
    ssm_b_im = nrm(ks[12], (DEPTH, SSM_GROUPS, SSM_STATE, SSM_GROUP), (2 * SSM_GROUP) ** -0.5)
    ssm_c_re = nrm(ks[13], (DEPTH, SSM_GROUPS, SSM_GROUP, SSM_STATE), (2 * SSM_STATE) ** -0.5)
    ssm_c_im = nrm(ks[14], (DEPTH, SSM_GROUPS, SSM_GROUP, SSM_STATE), (2 * SSM_STATE) ** -0.5)
    ssm_d = nrm(ks[15], (DEPTH, SSM_GROUPS, SSM_GROUP), 1.0)
    w_glu = nrm(ks[16], (DEPTH, SSM_WIDTH, SSM_WIDTH), SSM_WIDTH ** -0.5)
    b_glu = nrm(ks[17], (DEPTH, SSM_WIDTH), 0.01)
    diff_lq1 = nrm(ks[18], (DEPTH, DIFF_HEAD_DIM), 0.1)
    diff_lk1 = nrm(ks[19], (DEPTH, DIFF_HEAD_DIM), 0.1)
    diff_lq2 = nrm(ks[20], (DEPTH, DIFF_HEAD_DIM), 0.1)
    diff_lk2 = nrm(ks[21], (DEPTH, DIFF_HEAD_DIM), 0.1)
    diff_subln = 1.0 + nrm(ks[22], (DEPTH, DIFF_V_DIM), 0.02)
    return {"x": x, "mem": mem, "positions": positions,
            "norm_pre": norm_pre, "norm_post": norm_post, "norm_mem": norm_mem,
            "w_in": w_in, "w_out": w_out, "w_mem_kv": w_mem_kv,
            "ssm_a_re": ssm_a_re, "ssm_a_im": ssm_a_im, "ssm_log_dt": ssm_log_dt,
            "ssm_b_re": ssm_b_re, "ssm_b_im": ssm_b_im, "ssm_c_re": ssm_c_re, "ssm_c_im": ssm_c_im,
            "ssm_d": ssm_d, "w_glu": w_glu, "b_glu": b_glu,
            "diff_lq1": diff_lq1, "diff_lk1": diff_lk1, "diff_lq2": diff_lq2, "diff_lk2": diff_lk2,
            "diff_subln": diff_subln}

def first_block(x, mem, positions, norm_pre, norm_post, norm_mem, w_in, w_out, w_mem_kv,
              ssm_a_re, ssm_a_im, ssm_log_dt, ssm_b_re, ssm_b_im, ssm_c_re, ssm_c_im,
              ssm_d, w_glu, b_glu, diff_lq1, diff_lk1, diff_lq2, diff_lk2, diff_subln):
    bsz, seq = x.shape[0], x.shape[1]
    cos, sin = rope_tables(positions, DIFF_HEAD_DIM)
    widths = [SSM_WIDTH, SSM_WIDTH, DIFF_WIDTH, DIFF_WIDTH, DIFF_WIDTH, DIFF_WIDTH,
              XATTN_WIDTH, XATTN_WIDTH]
    split_at = [sum(widths[:i + 1]) for i in range(len(widths) - 1)]
    for l in range(DEPTH):
        lambda_init = 0.8 - 0.6 * math.exp(-0.3 * l)
        h = rmsnorm(x, norm_pre[l])
        proj = h @ w_in[l]
        u_s, g_s, q_d, k_d, v_d, g_d, q_x, g_x = jnp.split(proj, split_at, axis=-1)

        y_s = s5_scan(u_s, ssm_a_re[l], ssm_a_im[l], ssm_log_dt[l], ssm_b_re[l], ssm_b_im[l],
                      ssm_c_re[l], ssm_c_im[l], ssm_d[l])
        y_s = jax.nn.gelu(y_s)
        y_s = y_s * jax.nn.sigmoid(y_s @ w_glu[l] + b_glu[l])
        y_s = y_s * jax.nn.silu(g_s)

        q = apply_rope(q_d.reshape(bsz, seq, DIFF_HEADS, 2, DIFF_HEAD_DIM), cos, sin)
        k = apply_rope(k_d.reshape(bsz, seq, DIFF_HEADS, 2, DIFF_HEAD_DIM), cos, sin)
        v = v_d.reshape(bsz, seq, DIFF_HEADS, DIFF_V_DIM)
        lam = (jnp.exp(jnp.sum(diff_lq1[l].astype(jnp.float32) * diff_lk1[l].astype(jnp.float32)))
               - jnp.exp(jnp.sum(diff_lq2[l].astype(jnp.float32) * diff_lk2[l].astype(jnp.float32)))
               + lambda_init)
        y_d = diff_attention(q, k, v, lam, lambda_init, diff_subln[l]) * jax.nn.silu(g_d)

        mem_n = rmsnorm(mem, norm_mem[l])
        y_x = memory_attention(q_x.reshape(bsz, seq, XATTN_HEADS, XATTN_HEAD_DIM), mem_n, w_mem_kv[l])
        y_x = y_x * jax.nn.silu(g_x)

        mix = jnp.concatenate([y_s, y_d, y_x], axis=-1) @ w_out[l]
        x = x + rmsnorm(mix, norm_post[l])
    return x


_first_inputs = first_inputs


def first_inputs(seed=0):
    import zlib

    import numpy as np

    out = dict(_first_inputs(seed))
    spreads = {}
    factors = {'norm_post': 37.158,
     'norm_mem': 33.115,
     'ssm_a_re': 200.0,
     'ssm_b_re': 126.744,
     'ssm_b_im': 127.024,
     'ssm_c_re': 125.504,
     'ssm_c_im': 127.832,
     'b_glu': 200.0,
     'diff_subln': 117.978,
     'ssm_a_im': 26.104,
     'ssm_log_dt': 28.104,
     'w_glu': 14.215,
     'ssm_d': 3.027}
    for name, (base, spread) in spreads.items():
        noise = np.random.default_rng([zlib.crc32(name.encode()), seed]).standard_normal(out[name].shape)
        drawn = base * np.exp(spread * noise) if base else spread * noise
        out[name] = __import__('jax').numpy.asarray(drawn.astype(out[name].dtype))
    for name, factor in factors.items():
        out[name] = (out[name] * factor).astype(out[name].dtype)
    return out


_narrow_inputs = first_inputs


def first_inputs(seed=0):

    out = dict(_narrow_inputs(seed))
    wider = {'norm_post': 3.31, 'ssm_d': 3.3, 'w_glu': 4.13, 'b_glu': 12.0, 'diff_subln': 4.02}
    for name, times in wider.items():
        mean = out[name].mean()
        out[name] = (mean + times * (out[name] - mean)).astype(out[name].dtype)
    return out


DEPTH_2 = 2

CTX_LEN = 256
GRID_W = 64
D_MIX_2 = D_MODEL
HEAD_DIM = 128
ATTN_W = D_MIX_2 // 2
N_HEADS = ATTN_W // HEAD_DIM
N_KV_HEADS = 2
GQA_GROUP = N_HEADS // N_KV_HEADS
KV_W = N_KV_HEADS * HEAD_DIM
POOL_W = D_MIX_2 // 4
POOL_WINDOWS = (2, 4, 8, 16)
POOL_GROUPS = len(POOL_WINDOWS)
POOL_GC = POOL_W // POOL_GROUPS
FOURIER_W = D_MIX_2 - ATTN_W - POOL_W
FOURIER_GROUPS = 4
FOURIER_GC = FOURIER_W // FOURIER_GROUPS
OFF_Q = 0
OFF_K = OFF_Q + ATTN_W
OFF_V = OFF_K + KV_W
OFF_POOL = OFF_V + KV_W
OFF_FOURIER = OFF_POOL + POOL_W
OFF_GATE = OFF_FOURIER + FOURIER_W
IN_W = OFF_GATE + D_MIX_2
AXIS_ROT = HEAD_DIM // 2
EPS = 1e-6


def rmsnorm_2(x, g):
    xf = x.astype(jnp.float32)
    y = xf * lax.rsqrt(jnp.mean(xf * xf, axis=-1, keepdims=True) + EPS)
    return (y * g.astype(jnp.float32)).astype(x.dtype)

def axial_rope_tables(n):
    rows_count = n // GRID_W
    row = jnp.broadcast_to(jnp.arange(rows_count, dtype=jnp.float32)[:, None], (rows_count, GRID_W)).reshape(-1)
    col = jnp.broadcast_to(jnp.arange(GRID_W, dtype=jnp.float32)[None, :], (rows_count, GRID_W)).reshape(-1)
    inv = ROPE_THETA ** (-jnp.arange(0, AXIS_ROT, 2, dtype=jnp.float32) / AXIS_ROT)
    ang = jnp.stack([row[:, None] * inv, col[:, None] * inv], axis=1)
    return jnp.cos(ang), jnp.sin(ang)

def apply_axial_rope(x, cos, sin):
    B, N, H, _ = x.shape
    xr = x.astype(jnp.float32).reshape(B, N, H, 2, 2, AXIS_ROT // 2)
    x1, x2 = xr[..., 0, :], xr[..., 1, :]
    c = cos[None, :, None]
    s = sin[None, :, None]
    out = jnp.stack([x1 * c - x2 * s, x2 * c + x1 * s], axis=-2)
    return out.reshape(B, N, H, HEAD_DIM).astype(x.dtype)

def attend(qg, keys, vals):
    s = jnp.einsum('bqkgd,bskd->bkgqs', qg, keys, preferred_element_type=jnp.float32) * (HEAD_DIM ** -0.5)
    p = jax.nn.softmax(s, axis=-1).astype(vals.dtype)
    return jnp.einsum('bkgqs,bskd->bqkgd', p, vals)

def latent_attention(q, k, v, kc, vc):
    B, N = q.shape[:2]
    keys = jnp.concatenate([kc, k], axis=1)
    vals = jnp.concatenate([vc, v], axis=1)
    nb = N // Q_BLOCK
    qb = q.reshape(B, nb, Q_BLOCK, N_KV_HEADS, GQA_GROUP, HEAD_DIM).transpose(1, 0, 2, 3, 4, 5)
    o = lax.map(lambda qi: attend(qi, keys, vals), qb)
    return o.transpose(1, 0, 2, 3, 4, 5).reshape(B, N, ATTN_W)

def context_attention(qc, kc, vc):
    B, C = qc.shape[:2]
    qg = qc.reshape(B, C, N_KV_HEADS, GQA_GROUP, HEAD_DIM)
    return attend(qg, kc, vc).reshape(B, C, ATTN_W)

def multiscale_pool(u, pool_w, pool_scale):
    B, N, _ = u.shape
    uf = u.astype(jnp.float32).reshape(B, N, POOL_GROUPS, POOL_GC)
    cs = jnp.concatenate([jnp.zeros((B, 1, POOL_GROUPS, POOL_GC), jnp.float32), jnp.cumsum(uf, axis=1)], axis=1)
    t = jnp.arange(N, dtype=jnp.int32)
    outs = []
    for gi, win in enumerate(POOL_WINDOWS):
        lo = jnp.clip(t - win // 2, 0, N - 1)
        hi = jnp.clip(t + (win - win // 2) - 1, 0, N - 1)
        cnt = (hi - lo + 1).astype(jnp.float32)
        csg = cs[:, :, gi]
        win_sum = jnp.take(csg, hi + 1, axis=1) - jnp.take(csg, lo, axis=1)
        outs.append(win_sum / cnt[None, :, None] - uf[:, :, gi])
    pooled = jnp.stack(outs, axis=2).astype(u.dtype)
    y = jnp.einsum('bngc,gcd->bngd', pooled, pool_w).reshape(B, N, POOL_W)
    return y * pool_scale

def fourier_mix(u, fourier_w):
    B, N, _ = u.shape
    uf = u.astype(jnp.float32).reshape(B, N, FOURIER_GROUPS, FOURIER_GC)
    f = jnp.fft.fft2(uf, axes=(1, 3), norm='ortho').real.astype(u.dtype)
    return jnp.einsum('bngc,gcd->bngd', f, fourier_w).reshape(B, N, FOURIER_W)

def split_proj(p):
    return (p[..., OFF_Q:OFF_K], p[..., OFF_K:OFF_V], p[..., OFF_V:OFF_POOL],
            p[..., OFF_POOL:OFF_FOURIER], p[..., OFF_FOURIER:OFF_GATE], p[..., OFF_GATE:])

def merge_branches(att, u_pool, u_four, g, pool_w, pool_scale, fourier_w, w_out):
    mixed = jnp.concatenate([att, multiscale_pool(u_pool, pool_w, pool_scale), fourier_mix(u_four, fourier_w)], axis=-1)
    return (mixed * jax.nn.silu(g)) @ w_out

def second_inputs(seed: int = 0) -> dict:
    key = jax.random.key(seed)
    ks = jax.random.split(key, 20)
    f32 = jnp.float32
    nrm = lambda k, shape: jax.random.normal(k, shape, f32)
    return {
        "x": nrm(ks[0], (BATCH, SEQ, D_MODEL)),
        "c": nrm(ks[1], (BATCH, D_MODEL)),
        "ctx": nrm(ks[2], (BATCH, CTX_LEN, D_MODEL)),
        "c_ctx": nrm(ks[3], (D_MODEL,)),
        "ada_w": nrm(ks[4], (DEPTH_2, D_MODEL, 3 * D_MODEL)) * (0.5 * D_MODEL ** -0.5),
        "ada_b": nrm(ks[5], (DEPTH_2, 3 * D_MODEL)) * 0.01,
        "norm_g": 1.0 + 0.02 * nrm(ks[6], (DEPTH_2, D_MODEL)),
        "w_in": nrm(ks[7], (DEPTH_2, D_MODEL, IN_W)) * (D_MODEL ** -0.5),
        "q_norm_g": 1.0 + 0.02 * nrm(ks[8], (DEPTH_2, HEAD_DIM)),
        "k_norm_g": 1.0 + 0.02 * nrm(ks[9], (DEPTH_2, HEAD_DIM)),
        "pool_w": nrm(ks[10], (DEPTH_2, POOL_GROUPS, POOL_GC, POOL_GC)) * (POOL_GC ** -0.5),
        "pool_scale": 1.0 + 0.02 * nrm(ks[11], (DEPTH_2, POOL_W)),
        "fourier_w": nrm(ks[12], (DEPTH_2, FOURIER_GROUPS, FOURIER_GC, FOURIER_GC)) * (FOURIER_GC ** -0.5),
        "w_out": nrm(ks[13], (DEPTH_2, D_MIX_2, D_MODEL)) * (D_MIX_2 ** -0.5),
        "final_norm_g": 1.0 + 0.02 * nrm(ks[14], (D_MODEL,)),
    }

def second_block(x, c, ctx, c_ctx, ada_w, ada_b, norm_g, w_in, q_norm_g, k_norm_g,
              pool_w, pool_scale, fourier_w, w_out, final_norm_g):
    B, N, _ = x.shape
    C = ctx.shape[1]
    cos, sin = axial_rope_tables(N)
    xc = ctx
    for l in range(DEPTH_2):
        last = l == DEPTH_2 - 1
        shift, scale, gate = jnp.split(jax.nn.silu(c) @ ada_w[l] + ada_b[l], 3, axis=-1)
        shift_c, scale_c, gate_c = jnp.split(jax.nn.silu(c_ctx) @ ada_w[l] + ada_b[l], 3, axis=-1)
        h = rmsnorm_2(x, norm_g[l]) * (1.0 + scale[:, None]) + shift[:, None]
        hc = rmsnorm_2(xc, norm_g[l]) * (1.0 + scale_c) + shift_c

        if last:
            pkv = hc @ w_in[l][:, OFF_K:OFF_POOL]
            kc, vc = pkv[..., :KV_W], pkv[..., KV_W:]
        else:
            qc, kc, vc, upc, ufc, gc = split_proj(hc @ w_in[l])
        kc = rmsnorm_2(kc.reshape(B, C, N_KV_HEADS, HEAD_DIM), k_norm_g[l])
        vc = vc.reshape(B, C, N_KV_HEADS, HEAD_DIM)

        q, k, v, up, uf, g = split_proj(h @ w_in[l])
        q = apply_axial_rope(rmsnorm_2(q.reshape(B, N, N_HEADS, HEAD_DIM), q_norm_g[l]), cos, sin)
        k = apply_axial_rope(rmsnorm_2(k.reshape(B, N, N_KV_HEADS, HEAD_DIM), k_norm_g[l]), cos, sin)
        v = v.reshape(B, N, N_KV_HEADS, HEAD_DIM)
        att = latent_attention(q, k, v, kc, vc)
        out = merge_branches(att, up, uf, g, pool_w[l], pool_scale[l], fourier_w[l], w_out[l])
        x_new = x + gate[:, None] * out

        if not last:
            qc = rmsnorm_2(qc.reshape(B, C, N_HEADS, HEAD_DIM), q_norm_g[l])
            attc = context_attention(qc, kc, vc)
            outc = merge_branches(attc, upc, ufc, gc, pool_w[l], pool_scale[l], fourier_w[l], w_out[l])
            xc = xc + gate_c * outc
        x = x_new
    return rmsnorm_2(x, final_norm_g)


def setup_inputs(seed=0):
    out = dict(first_inputs(seed))
    for name, value in second_inputs(seed + 1).items():
        if name != "x":
            out[name + "_2"] = value
    return out


def reference(
    x, mem, positions, norm_pre, norm_post, norm_mem, w_in, w_out, w_mem_kv, ssm_a_re, ssm_a_im,
    ssm_log_dt, ssm_b_re, ssm_b_im, ssm_c_re, ssm_c_im, ssm_d, w_glu, b_glu, diff_lq1, diff_lk1,
    diff_lq2, diff_lk2, diff_subln, c_2, ctx_2, c_ctx_2, ada_w_2, ada_b_2, norm_g_2, w_in_2,
    q_norm_g_2, k_norm_g_2, pool_w_2, pool_scale_2, fourier_w_2, w_out_2, final_norm_g_2,
):
    x = first_block(
        x, mem, positions, norm_pre, norm_post, norm_mem, w_in, w_out, w_mem_kv, ssm_a_re,
        ssm_a_im, ssm_log_dt, ssm_b_re, ssm_b_im, ssm_c_re, ssm_c_im, ssm_d, w_glu, b_glu,
        diff_lq1, diff_lk1, diff_lq2, diff_lk2, diff_subln,
    )
    return second_block(
        x, c_2, ctx_2, c_ctx_2, ada_w_2, ada_b_2, norm_g_2, w_in_2, q_norm_g_2, k_norm_g_2,
        pool_w_2, pool_scale_2, fourier_w_2, w_out_2, final_norm_g_2,
    )


_drawn_inputs = setup_inputs


def setup_inputs(seed=0):
    import zlib

    import numpy as np

    out = dict(_drawn_inputs(seed))
    spreads = {}
    factors = {'b_glu': 4.925,
     'c_2': 8.0,
     'ctx_2': 8.0,
     'c_ctx_2': 8.0,
     'ada_w_2': 8.0,
     'ada_b_2': 53.067,
     'norm_g_2': 8.0,
     'w_in_2': 8.0,
     'q_norm_g_2': 64.0,
     'k_norm_g_2': 64.0,
     'pool_w_2': 8.0,
     'pool_scale_2': 8.0,
     'fourier_w_2': 8.0,
     'w_out_2': 8.0,
     'final_norm_g_2': 7.946}
    for name, (base, spread) in spreads.items():
        noise = np.random.default_rng([zlib.crc32(name.encode()), seed]).standard_normal(out[name].shape)
        drawn = base * np.exp(spread * noise) if base else spread * noise
        out[name] = __import__('jax').numpy.asarray(drawn.astype(out[name].dtype))
    for name, factor in factors.items():
        out[name] = (out[name] * factor).astype(out[name].dtype)
    return out
```

```python
import math
from contextlib import ExitStack

import numpy as np
import concourse.bass as bass
from concourse import mybir

F32 = mybir.dt.float32
F32R = mybir.dt.float32r
I32 = mybir.dt.int32
ALU = mybir.AluOpType
ACT = mybir.ActivationFunctionType
AX = mybir.AxisListType

P = 128
D = 2048
KC = D // P
T = 512
CT = 256
W = T + CT
TB = T // P
IN1 = 5120 // P
IN2 = 4608 // P
SSM_TILES = 32
SSM_CH = 8
S_FINE, S_COARSE = 32, 16
EPS = 1e-6
LAMBDA_INIT = 0.8 - 0.6 * math.exp(0.0)
MASK = -1e30
LAYERS = 2
HEADS2, KV2 = 8, 2

COLS = {}
NCOL = 0
for _name, _n in (("norm_pre", 16), ("norm_post", 16), ("norm_mem", 16), ("norm_g", 32), ("final", 16),
                  ("qk_gain", 20), ("pool_scale", 8), ("b_glu", 8), ("ssm_d", 8), ("subln", 1),
                  ("ada_b", 96), ("cond", 32), ("lam", 4), ("a_re", 32), ("a_im", 32), ("log_dt", 32),
                  ("inv_freq", 1)):
    COLS[_name] = NCOL
    NCOL += _n


CREDIT = 4


class Count:

    def __init__(self, handle):
        self.h, self.base = handle, CREDIT

    def at(self, n):
        return self.base + n


class Steps:

    def __init__(self, eng, count):
        self.eng, self.count = eng, count
        self.n = count.base
        self.steps = 0
        self.sem, self.now = count.h, self.n

    def step(self):
        self.n = self.n + 1
        self.steps += 1
        self.sem, self.now = self.count.h, self.n
        return self.sem

    def tell(self, count, n):
        self.sem, self.now = count.h, count.at(n)
        return self.sem

    def loop(self, times, body, lag=False, missing=0):
        n0, self.steps = self.n, 0
        body(0)
        head = self.steps
        per = head * 4 // 3 if lag else head + missing
        if times > 1:
            with self.eng.Fori(1, times) as i:
                self.n = i * per + (n0 + head - per) if per else n0
                self.sem, self.now = self.count.h, self.n
                self.steps = 0
                body(i)
                assert self.steps == per
        self.n = n0 + head + per * (times - 1)
        self.sem, self.now = self.count.h, self.n

    def end(self):
        self.count.base = self.n


def first(i):
    return isinstance(i, int) and i == 0


def row(ap, n):
    if isinstance(n, int):
        return ap[n]
    return ap[bass.ds(n, 1)].rearrange("a p n -> (a p) n")


def program(nc, cp, const, rope2, cn_sn, cs, invcnt, pos, x_in, mem_in, ctx_in, w_in, w_mem, w_glu,
            w_out, w_in2, w_out2, ada_w, ssm_b, ssm_c, pool_w, four_w, out):
    ctx = ExitStack()
    with ctx:
        def sb(name, shape, dt=F32):
            return ctx.enter_context(nc.sbuf_tensor(name, shape, dt))

        counts = []

        def count(name):
            counts.append(Count(ctx.enter_context(nc.semaphore(name))))
            return counts[-1]

        def dram(name, shape):
            return nc.dram_tensor(name, shape, F32, kind="Internal").ap()

        h_hi = sb("h_hi", [P, KC, W], F32R)
        h_lo = sb("h_lo", [P, KC, W], F32R)
        w_hi = sb("w_hi", [P, 2, D], F32R)
        w_lo = sb("w_lo", [P, 2, D], F32R)
        raw = sb("raw", [P, 4, D])
        xw = sb("xw", [P, KC * W])
        ident = sb("ident_sb", [P, P])
        rot = sb("rot_sb", [P, P])
        ones = sb("ones_sb", [P, P])
        cv = sb("cv", [P, NCOL])
        mods = sb("mods", [P, LAYERS, 48, 2])
        wide = sb("wide", [P, 3 * W])
        ssm_r = sb("ssm_r", [P, SSM_TILES])
        lam = sb("lam_sb", [P, 8])
        ccol = sb("ccol", [P, KC, 2])
        cst = sb("cst", [P, 4, 32])
        stat = sb("stat", [P, 32])
        raw1 = raw[:].rearrange("p a n -> p (a n)")
        xk = xw[:].rearrange("p (k n) -> p k n", k=KC)
        acc_sq, rstd, tmp = (wide[:, i * W:(i + 1) * W] for i in range(3))
        psum = [ctx.enter_context(nc.psum_tensor(f"ps{i}", [P, 1024], F32)) for i in range(4)]

        def bank(i):
            return psum[i // 2][:, (i % 2) * 512:(i % 2 + 1) * 512]

        proj = dram("proj", [IN1, P, T])
        mkv = dram("mkv", [8, P, CT])
        ys = dram("ys", [SSM_CH, P, T])
        proj2 = dram("proj2", [IN2, P, W])
        resid = dram("resid", [KC, P, W])
        mixd = dram("mixd", [8, P, W])
        four_m = dram("four_m", [LAYERS, P, 8 * P])
        ssm_e = dram("ssm_e", [SSM_CH, P, 4 * 2 * (S_FINE + S_COARSE)])
        ssm_cz = dram("ssm_cz", [SSM_CH, P, 4 * 2 * 32])

        def col(name, i=0):
            return cv[:, bass.ds(COLS[name] + i, 1)] if not isinstance(i, int) else \
                cv[:, COLS[name] + i:COLS[name] + i + 1]

        loaded = [count(f"loaded{i}") for i in range(8)]
        stored = [count(f"stored{i}") for i in range(4)]
        raw_full = [count(f"raw_full{i}") for i in range(4)]
        hi_done, lo_done = count("hi_done"), count("lo_done")
        w_used = count("w_used")
        acc_free = count("acc_free")
        acc_free_v = count("acc_free_v")
        staged = count("staged")
        va, vp, vv = count("steps_act"), count("steps_pool"), count("steps_vec")
        sq_ready, sq_summed = count("sq_ready"), count("sq_summed")
        sum_ready, rms_ready = count("sum_ready"), count("rms_ready")
        scaled, hi_ready = count("scaled"), count("hi_ready")
        e_ready, e_free = count("e_ready"), count("e_free")
        b_ready, b_read, x_ready, y_ready, y_out = (count(n) for n in
                                                    ("b_ready", "b_read", "x_ready", "y_ready", "y_out"))
        c_ready, ada_used, ada_added = (count(n) for n in ("c_ready", "ada_used", "ada_added"))
        s_ready, neg_max, exp_done, p_ready, t_ready, t_out, o_ready, o_read = (
            count(n) for n in ("s_ready", "neg_max", "exp_done", "p_ready", "t_ready", "t_out",
                               "o_ready", "o_read"))
        q_in, q_out = ([count(f"{n}{i}") for i in range(4)] for n in ("q_in", "q_out"))
        (rope_in, mix_in, sq_done, sums_done, root_done, qn_done, rot_done, rot_read, q_done, up_in, uf_in, cnt_in,
         pgate_in, fgate_in, pool_st, four_st, chan_done, y_copied, four_done, pooled, pool_done, p_tanh, f_tanh,
         pool_out, four_out, resid_in, resid_out, mixd_in, mixd_hi, mixd_lo) = (count(n) for n in (
             "rope_in", "mix_in", "sq_done", "sums_done", "root_done", "qn_done", "rot_done", "rot_read", "q_done",
             "up_in", "uf_in", "cnt_in", "pgate_in", "fgate_in", "pool_st", "four_st", "chan_done", "y_copied",
             "four_done", "pooled", "pool_done", "p_tanh", "f_tanh", "pool_out", "four_out", "resid_in", "resid_out",
             "mixd_in", "mixd_hi", "mixd_lo"))
        row_sums, sums_read, inverted = count("row_sums"), count("sums_read"), count("inverted")
        m1, m2, m3, m4, m5, m6 = (count(f"stage{i}") for i in range(1, 7))

        def linear(iters, wslot, nk, h0, segs, per_slot=1, store=None, act_out=None, vec_out=None,
                   stage_at=0, beside=None, keep=None):
            nslot = 4 * iters
            size = per_slot * nk * P
            blocks = [count_ for count_ in range(per_slot)]
            stage_w = sum(b - a for a, b in segs)
            off = [sum(b - a for a, b in segs[:q]) for q in range(len(segs))]

            def accs(par):
                return [bank(2 * par + q)[:, 0:b - a] for q, (a, b) in enumerate(segs)]

            def stage(par):
                return xw[:, stage_at + par * W:stage_at + par * W + stage_w]

            with nc.Block() as block:
                @block.sync
                def _(sp):
                    def body(i):
                        for j in range(4):
                            n = 4 * i + j
                            sp.wait_ge(hi_done.h, hi_done.at(n - 3))
                            sp.wait_ge(lo_done.h, lo_done.at(n - 3))
                            sp.dma_start(raw[:, j, 0:size], wslot(n)).then_inc(raw_full[j].h, 16)
                            if store and not (first(i) and j < 2):
                                sp.wait_ge(staged.h, staged.at(n - 1))
                                sp.dma_start(store(n - 2), stage((j - 2) % 4)).then_inc(stored[(j - 2) % 4].h, 16)
                            if keep and not (first(i) and j < 2):
                                sp.wait_ge(acc_free_v.h, acc_free_v.at(n - 1))
                                sp.dma_start(*keep(n - 2)).then_inc(resid_out.h, 16)
                            if beside and first(i) and j == 1:
                                beside(sp)
                    Steps(sp, vp).loop(iters, body)
                    if keep:
                        for n in (nslot - 2, nslot - 1):
                            sp.wait_ge(acc_free_v.h, acc_free_v.at(n + 1))
                            sp.dma_start(*keep(n)).then_inc(resid_out.h, 16)
                        sp.wait_ge(resid_out.h, resid_out.at(16 * nslot))
                    if store:
                        for n in (nslot - 2, nslot - 1):
                            sp.wait_ge(staged.h, staged.at(n + 1))
                            sp.dma_start(store(n), stage(n % 4)).then_inc(stored[n % 4].h, 16)
                        for q in range(4):
                            sp.wait_ge(stored[q].h, stored[q].at(16 * iters))

                @block.scalar
                def _(act):
                    st = Steps(act, va)

                    def read_out(n, par):
                        for e in blocks:
                            b = n * per_slot + e
                            act.wait_ge(w_used.h, w_used.at(b + 1))
                            if act_out:
                                act_out(st, b, accs((par * per_slot + e) % 2))
                            else:
                                act.wait_ge(stored[par].h, stored[par].at(4 * (n - par) if not isinstance(n, int) else 16 * (n // 4)))
                                for q, a in enumerate(accs(par % 2)):
                                    s = stage(par)[:, off[q]:off[q] + segs[q][1] - segs[q][0]]
                                    ins = act.activation(s, a, ACT.Copy)
                                ins.then_inc(staged.h, 1)

                    def body(i):
                        for j in range(4):
                            n = 4 * i + j
                            act.wait_ge(raw_full[j].h, raw_full[j].at(16 * (i + 1)))
                            act.wait_ge(w_used.h, w_used.at((n - 1) * per_slot))
                            act.activation(w_hi[:, j % 2, 0:size], raw[:, j, 0:size], ACT.Copy).then_inc(hi_done.h, 1)
                            if (act_out or store) and not (first(i) and j == 0):
                                read_out(n - 1, (j - 1) % 4)
                    st.loop(iters, body)
                    if act_out or store:
                        read_out(nslot - 1, 3)
                    st.end()

                @block.vector
                def _(dve):
                    st = Steps(dve, vv)

                    def read_out(n, par):
                        for e in blocks:
                            vec_out(st, n * per_slot + e, accs((par * per_slot + e) % 2))

                    def body(i):
                        for j in range(4):
                            n = 4 * i + j
                            dve.wait_ge(hi_done.h, hi_done.at(n + 1))
                            dve.tensor_tensor(w_lo[:, j % 2, 0:size], raw[:, j, 0:size],
                                              w_hi[:, j % 2, 0:size].bitcast(F32), ALU.subtract).then_inc(lo_done.h, 1)
                            if vec_out and not (first(i) and j == 0):
                                read_out(n - 1, (j - 1) % 4)
                    st.loop(iters, body, lag=True)
                    if vec_out:
                        read_out(nslot - 1, 3)
                    st.end()

                @block.tensor
                def _(pe):
                    def body(i):
                        for j in range(4):
                            n = 4 * i + j
                            pe.wait_ge(lo_done.h, lo_done.at(n + 1))
                            for e in blocks:
                                b = n * per_slot + e
                                a_ = accs((j * per_slot + e) % 2)
                                if store:
                                    pe.wait_ge(staged.h, staged.at(b - 1))
                                elif vec_out:
                                    pe.wait_ge(acc_free_v.h, acc_free_v.at(b - 1))
                                else:
                                    pe.wait_ge(acc_free.h, acc_free.at(b - 1))
                                for k in range(nk):
                                    wh = w_hi[:, j % 2, (e * nk + k) * P:(e * nk + k + 1) * P]
                                    wl = w_lo[:, j % 2, (e * nk + k) * P:(e * nk + k + 1) * P]
                                    for q, (lo, hi) in enumerate(segs):
                                        pe.matmul(a_[q], wh, h_hi[:, h0 + k, lo:hi], start=k == 0, stop=False)
                                        pe.matmul(a_[q], wh, h_lo[:, h0 + k, lo:hi], start=False, stop=False)
                                        ins = pe.matmul(a_[q], wl, h_hi[:, h0 + k, lo:hi], start=False, stop=k == nk - 1)
                                ins.then_inc(w_used.h, 1)
                    Steps(pe, vp).loop(iters, body)
            for r in raw_full:
                r.base += 16 * iters
            hi_done.base += nslot
            lo_done.base += nslot
            w_used.base += nslot * per_slot
            if store:
                staged.base += nslot
                for s in stored:
                    s.base += 16 * iters
            elif vec_out:
                acc_free_v.base += nslot * per_slot
            else:
                acc_free.base += nslot * per_slot

        def normalise(segs, from_acc, load=None, tail=None):
            lo_t, hi_t = segs[0][0], segs[-1][1]
            sq = [raw[:, q, 0:W] for q in range(4)]
            def low(dve, k):
                for q, (a, b, gain, shift) in enumerate(segs):
                    dve.wait_ge(hi_ready.h, hi_ready.at(k * len(segs) + q + 1))
                    if shift is None:
                        dve.tensor_tensor(h_lo[:, k, a:b], xk[:, k, a:b], h_hi[:, k, a:b].bitcast(F32), ALU.subtract)
                    else:
                        dve.scalar_tensor_tensor(h_lo[:, k, a:b], xk[:, k, a:b], shift(k),
                                                 h_hi[:, k, a:b].bitcast(F32), ALU.add, ALU.subtract)

            with nc.Block() as block:
                if load:
                    @block.sync
                    def _(sp):
                        load(sp)

                @block.scalar
                def _(act):
                    if not from_acc:
                        for k in range(KC):
                            if load:
                                act.wait_ge(loaded[k // 4].h, loaded[k // 4].at(32))
                            act.wait_ge(sq_summed.h, sq_summed.at(k - 3))
                            act.activation(sq[k % 4][:, lo_t:hi_t], xk[:, k, lo_t:hi_t], ACT.Square).then_inc(sq_ready.h, 1)
                    act.wait_ge(sum_ready.h, sum_ready.at(1))
                    act.activation(tmp[:, lo_t:hi_t], psum[0][:, lo_t:hi_t], ACT.Sqrt,
                                   bias=lam[:, 7:8], scale=1.0 / D).then_inc(rms_ready.h, 1)
                    for k in range(KC):
                        for q, (a, b, _, shift) in enumerate(segs):
                            act.wait_ge(scaled.h, scaled.at(k * len(segs) + q + 1))
                            if shift is None:
                                ins = act.activation(h_hi[:, k, a:b], xk[:, k, a:b], ACT.Copy)
                            else:
                                ins = act.activation(h_hi[:, k, a:b], xk[:, k, a:b], ACT.Identity, bias=shift(k))
                            ins.then_inc(hi_ready.h, 1)

                @block.vector
                def _(dve):
                    st = Steps(dve, vv)
                    if not from_acc:
                        for k in range(KC):
                            dve.wait_ge(sq_ready.h, sq_ready.at(k + 1))
                            if k == 0:
                                ins = dve.tensor_copy(acc_sq[:, lo_t:hi_t], sq[0][:, lo_t:hi_t])
                            else:
                                dve.wait_ge(sq_summed.h, sq_summed.at(k))
                                ins = dve.tensor_tensor(acc_sq[:, lo_t:hi_t], acc_sq[:, lo_t:hi_t],
                                                        sq[k % 4][:, lo_t:hi_t], ALU.add)
                            ins.then_inc(sq_summed.h, 1)
                    dve.wait_ge(rms_ready.h, rms_ready.at(1))
                    dve.reciprocal(rstd[:, lo_t:hi_t], tmp[:, lo_t:hi_t]).then_inc(st.step(), 1)
                    dve.wait_ge(st.sem, st.now)
                    g = 0
                    for k in range(KC):
                        for q, (a, b, gain, shift) in enumerate(segs):
                            dve.scalar_tensor_tensor(xk[:, k, a:b], xk[:, k, a:b], gain(k), rstd[:, a:b],
                                                     ALU.mult, ALU.mult).then_inc(scaled.h, 1)
                        if k:
                            low(dve, k - 1)
                    low(dve, KC - 1)
                    st.end()

                @block.tensor
                def _(pe):
                    if not from_acc:
                        pe.wait_ge(sq_summed.h, sq_summed.at(KC))
                    cuts = [(lo_t, min(hi_t, T))] + ([(T, hi_t)] if hi_t > T else [])
                    for a, b in cuts:
                        ins = pe.matmul(psum[0][:, a:b], ones[:], acc_sq[:, a:b], start=True, stop=True)
                    ins.then_inc(sum_ready.h, 1)
            if load:
                for g in range(4):
                    loaded[g].base += 32
            if not from_acc:
                sq_ready.base += KC
                sq_summed.base += KC
            sum_ready.base += 1
            rms_ready.base += 1
            scaled.base += KC * len(segs)
            hi_ready.base += KC * len(segs)

        def setup():
            with nc.Block() as block:
                @block.sync
                def _(sp):
                    for c in counts:
                        sp.sem_inc(c.h, CREDIT)
            with nc.Block() as block:
                @block.sync
                def _(sp):
                    sp.dma_start(ident[:], const[:, 0:P]).then_inc(m1.h, 16)
                    sp.dma_start(rot[:], const[:, P:2 * P]).then_inc(m1.h, 16)
                    sp.dma_start(cv[:], cp).then_inc(m1.h, 16)

                @block.vector
                def _(dve):
                    st = Steps(dve, vv)
                    dve.memset(ones[:], 1.0)
                    dve.memset(cst[:], 0.0)
                    dve.memset(lam[:, 7:8], EPS).then_inc(m2.h, 1)
                    dve.wait_ge(m1.h, m1.at(48))
                    l = COLS["lam"]
                    dve.tensor_tensor(lam[:, 0:2], cv[:, l:l + 2], cv[:, l + 2:l + 4], ALU.mult).then_inc(st.step(), 1)
                    dve.wait_ge(st.sem, st.now)
                    dve.tensor_scalar(lam[:, 2:4], lam[:, 0:2], 1.0, None, ALU.mult).then_inc(m3.h, 1)
                    dve.wait_ge(m4.h, m4.at(1))
                    c0 = COLS["cond"]
                    cflat = ccol[:].rearrange("p k s -> p (k s)")
                    dve.scalar_tensor_tensor(cflat, cflat, 1.0, cv[:, c0:c0 + 32], ALU.add, ALU.mult).then_inc(st.step(), 1)
                    dve.wait_ge(st.sem, st.now)
                    dve.tensor_scalar(cflat, cflat, 0.5, None, ALU.mult).then_inc(st.step(), 1)
                    dve.wait_ge(m5.h, m5.at(1))
                    dve.tensor_tensor(lam[:, 6:7], lam[:, 4:5], lam[:, 5:6], ALU.subtract).then_inc(st.step(), 1)
                    dve.wait_ge(st.sem, st.now)
                    dve.tensor_scalar(lam[:, 6:7], lam[:, 6:7], LAMBDA_INIT, None, ALU.add).then_inc(st.step(), 1)
                    for name, n, f in (("b_glu", 8, 0.5), ("pool_scale", 8, 0.5), ("subln", 1, 0.5 * (1.0 - LAMBDA_INIT))):
                        a = COLS[name]
                        dve.tensor_scalar(cv[:, a:a + n], cv[:, a:a + n], f, None, ALU.mult).then_inc(st.step(), 1)
                    dve.wait_ge(st.sem, st.now)
                    st.end()

                @block.scalar
                def _(act):
                    act.wait_ge(m1.h, m1.at(48))
                    c0 = COLS["cond"]
                    act.activation(ccol[:].rearrange("p k s -> p (k s)"), cv[:, c0:c0 + 32], ACT.Tanh, scale=0.5).then_inc(m4.h, 1)
                    act.wait_ge(m6.h, m6.at(1))
                    act.activation(lam[:, 4:6], psum[0][:, 0:2], ACT.Exp).then_inc(m5.h, 1)

                @block.tensor
                def _(pe):
                    pe.wait_ge(m2.h, m2.at(1))
                    pe.wait_ge(m3.h, m3.at(1))
                    pe.matmul(psum[0][:, 0:2], ones[:], lam[:, 2:4], start=True, stop=True).then_inc(m6.h, 1)
            m1.base += 48
            for m in (m2, m3, m4, m5, m6):
                m.base += 1

        def load_x_mem(sp):
            for g in range(4):
                sp.dma_start(xk[:, 4 * g:4 * g + 4, 0:T], x_in[:, 4 * g:4 * g + 4, :]).then_inc(loaded[g].h, 16)
                sp.dma_start(xk[:, 4 * g:4 * g + 4, T:W], mem_in[:, 4 * g:4 * g + 4, :]).then_inc(loaded[g].h, 16)

        def ssm_prepare():
            n = SSM_TILES
            at = [0]

            def take(size):
                at[0] += size
                return xw[:, at[0] - size:at[0]]
            (dt_, lrdt, th, k_, r_, s_, c_, are, aim, den, nr, t1, t2, zr, zi, wr, wi, wr2, wi2, mask) = (
                take(n) for _ in range(20))
            ew = S_FINE + S_COARSE
            e_sb = take(n * 2 * ew).rearrange("p (t c n) -> p t c n", t=n, c=2)
            big = [take(n * 16) for _ in range(2)]
            c_raw = take(n * 64).rearrange("p (t c h) -> p t c h", t=n, c=2)
            cz = take(n * 64).rearrange("p (t c h) -> p t c h", t=n, c=2)
            cb = [take(n * 32) for _ in range(2)]
            cs_sb = raw1[:, 0:2 * P]
            fw = [raw1[:, (1 + l) * T:(2 + l) * T] for l in range(LAYERS)]
            fm = [raw1[:, (3 + 2 * l) * T:(5 + 2 * l) * T].rearrange("p (g z d) -> p g z d", g=4, z=2) for l in range(LAYERS)]
            a_re, a_im, ldt = (cv[:, COLS[x]:COLS[x] + n] for x in ("a_re", "a_im", "log_dt"))
            two_pi = 2.0 * math.pi
            c1 = 6.28125
            c2 = 0.0019350051879882812
            c3 = two_pi - c1 - c2
            magic = 12582912.0
            with nc.Block() as block:
                @block.sync
                def _(sp):
                    sp.dma_start(c_raw.rearrange("p t c h -> p (t c h)"), ssm_c).then_inc(m1.h, 16)
                    sp.dma_start(cs_sb, cs).then_inc(mix_in.h, 16)
                    for l in range(LAYERS):
                        sp.dma_start(fw[l], four_w[l]).then_inc(mix_in.h, 16)
                        sp.wait_ge(y_copied.h, y_copied.at(l + 1))
                        sp.dma_start(four_m[l], fm[l].rearrange("p g z d -> p (g z d)")).then_inc(four_st.h, 16)
                    sp.wait_ge(four_st.h, four_st.at(32))
                    sp.wait_ge(m6.h, m6.at(1))
                    sp.dma_start(ssm_e.rearrange("c p n -> p c n"),
                                 e_sb.rearrange("p t c n -> p (t c n)").rearrange("p (c n) -> p c n", c=SSM_CH)).then_inc(m1.h, 16)
                    sp.dma_start(ssm_cz.rearrange("c p n -> p c n"),
                                 cz.rearrange("p t c n -> p (t c n)").rearrange("p (c n) -> p c n", c=SSM_CH)).then_inc(m1.h, 16)
                    sp.wait_ge(m1.h, m1.at(48))

                @block.tensor
                def _(pe):
                    for l in range(LAYERS):
                        pe.wait_ge(mix_in.h, mix_in.at(16 * (2 + l)))
                        pe.matmul(bank(2 * l), cs_sb[:, 0:P], fw[l], start=True, stop=True)
                        pe.matmul(bank(2 * l + 1), cs_sb[:, P:2 * P], fw[l], start=True, stop=True).then_inc(chan_done.h, 1)

                @block.scalar
                def _(act):
                    act.activation(dt_, ldt, ACT.Exp).then_inc(m2.h, 1)
                    act.wait_ge(m3.h, m3.at(1))
                    act.activation(ssm_r[:], lrdt, ACT.Exp).then_inc(m2.h, 1)
                    act.wait_ge(m3.h, m3.at(2))
                    act.activation(s_, r_, ACT.Sin).then_inc(m2.h, 1)
                    act.wait_ge(m3.h, m3.at(3))
                    act.activation(c_, r_, ACT.Sin).then_inc(m2.h, 1)
                    for l in range(LAYERS):
                        act.wait_ge(chan_done.h, chan_done.at(l + 1))
                        for z in range(2):
                            ins = act.activation(fm[l][:, :, z, :], bank(2 * l + z).rearrange("p (g d) -> p g d", g=4), ACT.Copy)
                        ins.then_inc(y_copied.h, 1)

                @block.vector
                def _(dve):
                    st = Steps(dve, vv)

                    def ts(out_, a, x1, x2, o1, o2=None):
                        dve.wait_ge(st.sem, st.now)
                        if o2 is None:
                            dve.tensor_scalar(out_, a, x1, None, o1).then_inc(st.step(), 1)
                        else:
                            dve.tensor_scalar(out_, a, x1, x2, o1, o2).then_inc(st.step(), 1)

                    def tt(out_, a, b, op):
                        dve.wait_ge(st.sem, st.now)
                        dve.tensor_tensor(out_, a, b, op).then_inc(st.step(), 1)

                    def stt(out_, a, x, b, o1, o2):
                        dve.wait_ge(st.sem, st.now)
                        dve.scalar_tensor_tensor(out_, a, x, b, o1, o2).then_inc(st.step(), 1)
                    dve.wait_ge(m2.h, m2.at(1))
                    tt(th, a_im, dt_, ALU.mult)
                    dve.wait_ge(st.sem, st.now)
                    dve.tensor_tensor(lrdt, a_re, dt_, ALU.mult).then_inc(st.tell(m3, 1), 1)
                    ts(k_, th, 1.0 / two_pi, magic, ALU.mult, ALU.add)
                    ts(k_, k_, -magic, None, ALU.add)
                    stt(r_, k_, -c1, th, ALU.mult, ALU.add)
                    stt(r_, k_, -c2, r_, ALU.mult, ALU.add)
                    stt(r_, k_, -c3, r_, ALU.mult, ALU.add)
                    dve.wait_ge(st.sem, st.now)
                    dve.tensor_scalar(r_, r_, 3.1415925, -3.1415925, ALU.min, ALU.max).then_inc(st.tell(m3, 2), 1)
                    dve.wait_ge(m2.h, m2.at(3))
                    ts(r_, r_, math.pi / 2, None, ALU.add)
                    ts(mask, r_, math.pi, -two_pi, ALU.is_gt, ALU.mult)
                    tt(r_, r_, mask, ALU.add)
                    dve.wait_ge(st.sem, st.now)
                    dve.tensor_scalar(r_, r_, 3.1415925, -3.1415925, ALU.min, ALU.max).then_inc(st.tell(m3, 3), 1)
                    dve.wait_ge(m2.h, m2.at(4))
                    tt(are, ssm_r[:], c_, ALU.mult)
                    tt(aim, ssm_r[:], s_, ALU.mult)
                    tt(den, a_re, a_re, ALU.mult)
                    tt(t1, a_im, a_im, ALU.mult)
                    tt(den, den, t1, ALU.add)
                    ts(nr, are, -1.0, None, ALU.add)
                    dve.wait_ge(st.sem, st.now)
                    dve.reciprocal(den, den).then_inc(st.step(), 1)
                    tt(t1, nr, a_re, ALU.mult)
                    tt(t2, aim, a_im, ALU.mult)
                    tt(t1, t1, t2, ALU.add)
                    tt(zr, t1, den, ALU.mult)
                    tt(t1, aim, a_re, ALU.mult)
                    tt(t2, nr, a_im, ALU.mult)
                    tt(t1, t1, t2, ALU.subtract)
                    tt(zi, t1, den, ALU.mult)
                    ts(wr, c_, 1.0, None, ALU.mult)
                    ts(wi, s_, 1.0, None, ALU.mult)

                    def table(lo, size):
                        er, ei = e_sb[:, :, 0, lo:lo + size], e_sb[:, :, 1, lo:lo + size]
                        dve.wait_ge(st.sem, st.now)
                        dve.memset(er[:, :, 0:1], 1.0).then_inc(st.step(), 1)
                        dve.wait_ge(st.sem, st.now)
                        dve.memset(ei[:, :, 0:1], 0.0).then_inc(st.step(), 1)
                        m = 1
                        while m < size:
                            br = wr.rearrange("p (t o) -> p t o", o=1).to_broadcast([P, n, m])
                            bi = wi.rearrange("p (t o) -> p t o", o=1).to_broadcast([P, n, m])
                            x1 = big[0][:, 0:n * m].rearrange("p (t m) -> p t m", m=m)
                            x2 = big[1][:, 0:n * m].rearrange("p (t m) -> p t m", m=m)
                            tt(x1, er[:, :, 0:m], br, ALU.mult)
                            tt(x2, ei[:, :, 0:m], bi, ALU.mult)
                            tt(er[:, :, m:2 * m], x1, x2, ALU.subtract)
                            tt(x1, er[:, :, 0:m], bi, ALU.mult)
                            tt(x2, ei[:, :, 0:m], br, ALU.mult)
                            tt(ei[:, :, m:2 * m], x1, x2, ALU.add)
                            tt(t1, wr, wr, ALU.mult)
                            tt(t2, wi, wi, ALU.mult)
                            tt(wr2, t1, t2, ALU.subtract)
                            tt(t1, wr, wi, ALU.mult)
                            ts(wi2, t1, 2.0, None, ALU.mult)
                            ts(wr, wr2, 1.0, None, ALU.mult)
                            ts(wi, wi2, 1.0, None, ALU.mult)
                            m *= 2
                    table(0, S_FINE)
                    table(S_FINE, S_COARSE)
                    dve.wait_ge(m1.h, m1.at(16))
                    zrb = zr.rearrange("p (t o) -> p t o", o=1).to_broadcast([P, n, 32])
                    zib = zi.rearrange("p (t o) -> p t o", o=1).to_broadcast([P, n, 32])
                    x1, x2 = (b_.rearrange("p (t h) -> p t h", h=32) for b_ in cb)
                    tt(x1, c_raw[:, :, 0, :], zrb, ALU.mult)
                    tt(x2, c_raw[:, :, 1, :], zib, ALU.mult)
                    tt(cz[:, :, 0, :], x1, x2, ALU.subtract)
                    tt(x1, c_raw[:, :, 0, :], zib, ALU.mult)
                    tt(x2, c_raw[:, :, 1, :], zrb, ALU.mult)
                    tt(x1, x1, x2, ALU.add)
                    dve.wait_ge(st.sem, st.now)
                    dve.tensor_scalar(cz[:, :, 1, :], x1, -1.0, None, ALU.mult).then_inc(st.tell(m6, 1), 1)
                    st.end()
            mix_in.base += 48
            chan_done.base += 2
            y_copied.base += 2
            four_st.base += 32
            m1.base += 48
            m2.base += 4
            m3.base += 3
            m6.base += 1

        def ssm_half(l):
            at = [0]

            def take(size):
                at[0] += size
                return xw[:, at[0] - size:at[0]]
            ee = [[take(T) for _ in range(2)] for _ in range(2)]
            gt = [take(T) for _ in range(4)]
            t = [take(T) for _ in range(6)]
            xr, xi, u = take(T), take(T), take(T)
            b_sb = take(4 * 2 * P).rearrange("p (j c s) -> p j c s", j=4, c=2)
            cz = take(4 * 2 * 32).rearrange("p (j c h) -> p j c h", j=4, c=2)
            e_sb = take(4 * 2 * (S_FINE + S_COARSE)).rearrange("p (j c n) -> p j c n", j=4, c=2)
            yst = take(T)
            stg = [take(T) for _ in range(2)]
            ada_acc = wide[:, 0:3 * T]
            acc = [bank(0), bank(1)]
            b_ps = [bank(2), bank(3)]
            y_ps = bank(4)
            ada_ps = [bank(5), bank(6), bank(7)]
            block0 = 8 + 16 * l

            with nc.Block() as block:
                @block.sync
                def _(sp):
                    def body(i):
                        sp.wait_ge(b_ready.h, b_ready.at(4 * i))
                        sp.dma_start(b_sb.rearrange("p j c s -> p (j c s)"), row(ssm_b, i + 4 * l)).then_inc(loaded[0].h, 16)
                        sp.dma_start(u, row(proj, i + 4 * l)).then_inc(loaded[0].h, 16)
                        sp.wait_ge(e_ready.h, e_ready.at(4 * i))
                        sp.dma_start(e_sb.rearrange("p j c n -> p (j c n)"), row(ssm_e, i + 4 * l)).then_inc(loaded[1].h, 16)
                        for j in range(4):
                            n = 4 * i + j
                            if j == 1:
                                sp.wait_ge(y_ready.h, y_ready.at(4 * i))
                                sp.dma_start(cz.rearrange("p j c h -> p (j c h)"), row(ssm_cz, i + 4 * l)).then_inc(loaded[2].h, 16)
                            sp.wait_ge(hi_done.h, hi_done.at(n))
                            sp.wait_ge(lo_done.h, lo_done.at(n))
                            sp.dma_start(raw[:, 0, :], row(w_in, n + block0)).then_inc(raw_full[0].h, 16)
                            for r in range(3):
                                sp.wait_ge(ada_used.h, ada_used.at(3 * n - 2 + r))
                                sp.dma_start(raw[:, 1 + r, :], ada_w[l, r](n)).then_inc(raw_full[1 + r].h, 16)
                            if not (first(i) and j < 2):
                                sp.wait_ge(staged.h, staged.at(n - 1))
                                sp.dma_start(row(proj, n - 2 + block0), stg[j % 2]).then_inc(stored[j % 2].h, 16)
                            if j == 0 and not first(i):
                                sp.wait_ge(y_out.h, y_out.at(i))
                                sp.dma_start(row(ys, i - 1 + 4 * l), yst).then_inc(stored[2].h, 16)
                    Steps(sp, vp).loop(4, body)
                    for n in (14, 15):
                        sp.wait_ge(staged.h, staged.at(n + 1))
                        sp.dma_start(row(proj, n + block0), stg[n % 2]).then_inc(stored[n % 2].h, 16)
                    sp.wait_ge(y_out.h, y_out.at(4))
                    sp.dma_start(row(ys, 3 + 4 * l), yst).then_inc(stored[2].h, 16)
                    sp.wait_ge(stored[0].h, stored[0].at(16 * 8))
                    sp.wait_ge(stored[1].h, stored[1].at(16 * 8))
                    sp.wait_ge(stored[2].h, stored[2].at(16 * 4))

                @block.gpsimd
                def _(pool):
                    st = Steps(pool, vp)

                    def body(i):
                        pool.wait_ge(loaded[1].h, loaded[1].at(16 * (i + 1)))
                        for j in range(4):
                            n = 4 * i + j
                            pool.wait_ge(e_free.h, e_free.at(n - 1))
                            f_re, f_im = (e_sb[:, j, c, 0:S_FINE].rearrange("p (o s) -> p o s", o=1)
                                          .to_broadcast([P, S_COARSE, S_FINE]) for c in range(2))
                            c_re, c_im = (e_sb[:, j, c, S_FINE:].rearrange("p (s o) -> p s o", o=1)
                                          .to_broadcast([P, S_COARSE, S_FINE]) for c in range(2))
                            g_ = [x.rearrange("p (a b) -> p a b", b=S_FINE) for x in gt]
                            pool.wait_ge(st.sem, st.now)
                            for q, (a, b) in enumerate(((f_re, c_re), (f_im, c_im), (f_re, c_im), (f_im, c_re))):
                                pool.tensor_tensor(g_[q], a, b, ALU.mult).then_inc(st.step(), 1)
                            pool.wait_ge(st.sem, st.now)
                            pool.tensor_tensor(ee[j % 2][0], gt[0], gt[1], ALU.subtract).then_inc(st.step(), 1)
                            pool.wait_ge(st.sem, st.now)
                            pool.tensor_tensor(ee[j % 2][1], gt[2], gt[3], ALU.add).then_inc(st.tell(e_ready, n + 1), 1)
                    st.loop(4, body)
                    st.end()

                @block.scalar
                def _(act):
                    st = Steps(act, va)

                    def body(i):
                        act.wait_ge(ada_used.h, ada_used.at(12 * i))
                        act.activation(cst[:, :, 0:2], ccol[:].rearrange("p k s -> p (k s)")[:, bass.ds(i * 8, 8)]
                                       .rearrange("p (k s) -> p k s", s=2) if not isinstance(i, int) else
                                       ccol[:, 4 * i:4 * i + 4, :], ACT.Copy).then_inc(c_ready.h, 1)
                        for j in range(4):
                            n = 4 * i + j
                            act.wait_ge(raw_full[0].h, raw_full[0].at(16 * (n + 1)))
                            act.wait_ge(w_used.h, w_used.at(n - 1))
                            act.activation(w_hi[:, j % 2, :], raw[:, 0, :], ACT.Copy).then_inc(hi_done.h, 1)
                            if not (first(i) and j == 0):
                                out_(n - 1, (j - 1) % 2)
                            if j == 0 and not first(i):
                                y_copy(i - 1)

                    def out_(n, par):
                        act.wait_ge(w_used.h, w_used.at(n + 1))
                        if isinstance(n, int):
                            act.wait_ge(stored[par].h, stored[par].at(16 * (n // 2)))
                        else:
                            act.wait_ge(stored[par].h, stored[par].at(8 * (n - par)))
                        act.activation(stg[par], acc[par], ACT.Copy).then_inc(staged.h, 1)

                    def y_copy(c):
                        act.wait_ge(y_ready.h, y_ready.at(4 * c + 4))
                        act.wait_ge(stored[2].h, stored[2].at(16 * c))
                        act.activation(yst, y_ps, ACT.Copy).then_inc(y_out.h, 1)
                    st.loop(4, body)
                    out_(15, 1)
                    y_copy(3)
                    st.end()

                @block.vector
                def _(dve):
                    st = Steps(dve, vv)
                    dve.memset(ada_acc, 0.0).then_inc(st.step(), 1)

                    def body(i):
                        for j in range(4):
                            n = 4 * i + j
                            dve.wait_ge(hi_done.h, hi_done.at(n + 1))
                            dve.tensor_tensor(w_lo[:, j % 2, :], raw[:, 0, :], w_hi[:, j % 2, :].bitcast(F32),
                                              ALU.subtract).then_inc(lo_done.h, 1)
                            er, ei = ee[j % 2]
                            dve.wait_ge(b_ready.h, b_ready.at(n + 1))
                            dve.wait_ge(e_ready.h, e_ready.at(n + 1))
                            dve.tensor_tensor(t[0], b_ps[0], er, ALU.mult).then_inc(st.step(), 1)
                            dve.tensor_tensor(t[1], b_ps[1], ei, ALU.mult).then_inc(st.step(), 1)
                            dve.tensor_tensor(t[2], b_ps[1], er, ALU.mult).then_inc(st.step(), 1)
                            dve.tensor_tensor(t[3], b_ps[0], ei, ALU.mult).then_inc(st.tell(b_read, n + 1), 1)
                            dve.wait_ge(st.sem, st.now)
                            dve.tensor_tensor(t[4], t[0], t[1], ALU.add).then_inc(st.step(), 1)
                            dve.tensor_tensor(t[5], t[2], t[3], ALU.subtract).then_inc(st.step(), 1)
                            dve.wait_ge(st.sem, st.now)
                            if j == 3:
                                dve.wait_ge(ada_used.h, ada_used.at(12 * (i + 1)))
                                for r in range(3):
                                    ins = dve.tensor_tensor(ada_acc[:, r * T:(r + 1) * T], ada_acc[:, r * T:(r + 1) * T],
                                                            ada_ps[r], ALU.add)
                                    if r < 2:
                                        ins.then_inc(st.step(), 1)
                                    else:
                                        ins.then_inc(st.tell(ada_added, i + 1), 1)
                            mag = ssm_r[:, bass.ds(n + 16 * l, 1)] if not isinstance(n, int) else ssm_r[:, n + 16 * l:n + 16 * l + 1]
                            dve.tensor_tensor_scan(t[0], mag.to_broadcast([P, T]), t[4], 0.0, ALU.mult, ALU.add).then_inc(st.step(), 1)
                            dve.tensor_tensor_scan(t[1], mag.to_broadcast([P, T]), t[5], 0.0, ALU.mult, ALU.add).then_inc(st.step(), 1)
                            dve.wait_ge(st.sem, st.now)
                            dve.tensor_tensor(t[2], t[0], er, ALU.mult).then_inc(st.step(), 1)
                            dve.tensor_tensor(t[3], t[1], ei, ALU.mult).then_inc(st.step(), 1)
                            dve.tensor_tensor(t[4], t[0], ei, ALU.mult).then_inc(st.step(), 1)
                            dve.tensor_tensor(t[5], t[1], er, ALU.mult).then_inc(st.tell(e_free, n + 1), 1)
                            dve.wait_ge(st.sem, st.now)
                            dve.wait_ge(y_ready.h, y_ready.at(n))
                            dve.tensor_tensor(xr, t[2], t[3], ALU.subtract).then_inc(st.step(), 1)
                            dve.tensor_tensor(xi, t[4], t[5], ALU.add).then_inc(st.tell(x_ready, n + 1), 1)
                            dve.wait_ge(st.sem, st.now)
                    st.loop(4, body)
                    st.end()

                @block.tensor
                def _(pe):
                    def state_out(c, j, m):
                        pe.wait_ge(x_ready.h, x_ready.at(m + 1))
                        pe.wait_ge(loaded[2].h, loaded[2].at(16 * (c + 1)))
                        if j == 0:
                            pe.wait_ge(y_out.h, y_out.at(c))
                        yq = y_ps[32 * j:32 * j + 32, :]
                        pe.matmul(yq, cz[:, j, 0, :], xr, start=True, stop=False)
                        pe.matmul(yq, cz[:, j, 1, :], xi, start=False, stop=True).then_inc(y_ready.h, 1)

                    def body(i):
                        for j in range(4):
                            n = 4 * i + j
                            if j == 0:
                                pe.wait_ge(c_ready.h, c_ready.at(i + 1))
                                pe.wait_ge(ada_added.h, ada_added.at(i))
                            for r in range(3):
                                pe.wait_ge(raw_full[1 + r].h, raw_full[1 + r].at(16 * (n + 1)))
                                for q in range(4):
                                    ins = pe.matmul(ada_ps[r][32 * q:32 * q + 32, :], cst[:, j, :],
                                                    raw[:, 1 + r, q * T:(q + 1) * T], start=j == 0, stop=j == 3)
                                ins.then_inc(ada_used.h, 1)
                            pe.wait_ge(loaded[0].h, loaded[0].at(32 * (i + 1)))
                            pe.wait_ge(b_read.h, b_read.at(n))
                            pe.matmul(b_ps[0], b_sb[:, j, 0, :], u, start=True, stop=True)
                            pe.matmul(b_ps[1], b_sb[:, j, 1, :], u, start=True, stop=True).then_inc(b_ready.h, 1)
                            if j > 0:
                                state_out(i, j - 1, n - 1)
                            elif not first(i):
                                state_out(i - 1, 3, n - 1)
                            pe.wait_ge(lo_done.h, lo_done.at(n + 1))
                            pe.wait_ge(staged.h, staged.at(n - 1))
                            for k in range(KC):
                                wh = w_hi[:, j % 2, k * P:(k + 1) * P]
                                wl = w_lo[:, j % 2, k * P:(k + 1) * P]
                                pe.matmul(acc[j % 2], wh, h_hi[:, k, 0:T], start=k == 0, stop=False)
                                pe.matmul(acc[j % 2], wh, h_lo[:, k, 0:T], start=False, stop=False)
                                ins = pe.matmul(acc[j % 2], wl, h_hi[:, k, 0:T], start=False, stop=k == KC - 1)
                            ins.then_inc(w_used.h, 1)
                    Steps(pe, vp).loop(4, body)
                    state_out(3, 3, 15)
            for s, v in ((loaded[0], 128), (loaded[1], 64), (loaded[2], 64), (b_ready, 16), (b_read, 16), (e_ready, 16),
                         (e_free, 16), (x_ready, 16), (y_ready, 16), (y_out, 4), (c_ready, 4), (ada_used, 48),
                         (ada_added, 4), (hi_done, 16), (lo_done, 16), (w_used, 16), (staged, 16), (stored[0], 128),
                         (stored[1], 128), (stored[2], 64)):
                s.base += v
            for r in raw_full:
                r.base += 256

        def ada_finish(l):
            with nc.Block() as block:
                @block.tensor
                def _(pe):
                    for r in range(3):
                        for m in range(4):
                            ins = pe.transpose(bank(r)[:, m * P:(m + 1) * P], wide[:, r * T + m * P:r * T + (m + 1) * P], ident[:])
                        ins.then_inc(m1.h, 1)

                @block.vector
                def _(dve):
                    b0 = COLS["ada_b"] + 48 * l
                    for r in range(3):
                        dve.wait_ge(m1.h, m1.at(r + 1))
                        for s in range(2):
                            dve.tensor_tensor(
                                mods[:, l, 16 * r:16 * r + 16, s].rearrange("p (q m) -> p q m", q=4),
                                bank(r).rearrange("p (m q z) -> p q m z", m=4, q=4)[:, :, :, s],
                                cv[:, b0 + 16 * r:b0 + 16 * r + 16].rearrange("p (q m) -> p q m", q=4), ALU.add)
            m1.base += 3
            with nc.Block() as block:
                @block.vector
                def _(dve):
                    st = Steps(dve, vv)
                    sc = mods[:, l, 16:32, :]
                    dve.tensor_scalar(sc, sc, 1.0, None, ALU.add).then_inc(st.step(), 1)
                    dve.wait_ge(st.sem, st.now)
                    g0 = COLS["norm_g"] + 16 * l
                    for s in range(2):
                        dve.tensor_tensor(mods[:, l, 16:32, s], mods[:, l, 16:32, s], cv[:, g0:g0 + 16], ALU.mult).then_inc(st.step(), 1)
                    st.end()

        def glu():
            y_at = [xw[:, c * T:(c + 1) * T] for c in range(8)]
            g_at = [raw1[:, c * T:(c + 1) * T] for c in range(8)]
            ub = [xw[:, (8 + c) * T:(9 + c) * T] for c in range(8)]
            th = [xw[:, (16 + c) * T:(17 + c) * T] for c in range(4)]
            k0 = math.sqrt(2.0 / math.pi)
            with nc.Block() as block:
                @block.sync
                def _(sp):
                    for c in range(8):
                        sp.dma_start(y_at[c], ys[c]).then_inc(loaded[c].h, 16)
                        sp.dma_start(ub[c], proj[c]).then_inc(loaded[c].h, 16)
                        sp.dma_start(g_at[c], proj[8 + c]).then_inc(loaded[c].h, 16)

                @block.scalar
                def _(act):
                    for c in range(8):
                        act.wait_ge(m1.h, m1.at(c + 1))
                        act.activation(th[c % 2], ub[c], ACT.Tanh, scale=k0).then_inc(m2.h, 1)
                        act.activation(th[2 + c % 2], g_at[c], ACT.Tanh, scale=0.5).then_inc(m2.h, 1)
                        act.wait_ge(m3.h, m3.at(c + 1))
                        act.activation(h_hi[:, 8 + c, 0:T], y_at[c], ACT.Copy).then_inc(m4.h, 1)

                @block.vector
                def _(dve):
                    st = Steps(dve, vv)
                    for c in range(8):
                        dve.wait_ge(loaded[c].h, loaded[c].at(48))
                        y, ui = y_at[c], ub[c]
                        dve.scalar_tensor_tensor(y, ui, col("ssm_d", c), y, ALU.mult, ALU.add).then_inc(st.step(), 1)
                        dve.wait_ge(st.sem, st.now)
                        dve.tensor_tensor(ui, y, y, ALU.mult).then_inc(st.step(), 1)
                        dve.wait_ge(st.sem, st.now)
                        dve.tensor_scalar(ui, ui, 0.044715, 1.0, ALU.mult, ALU.add).then_inc(st.step(), 1)
                        dve.wait_ge(st.sem, st.now)
                        dve.tensor_tensor(ui, ui, y, ALU.mult).then_inc(st.tell(m1, c + 1), 1)
                        dve.wait_ge(m2.h, m2.at(2 * (c + 1)))
                        dve.scalar_tensor_tensor(y, th[c % 2], 1.0, y, ALU.add, ALU.mult).then_inc(st.step(), 1)
                        dve.wait_ge(st.sem, st.now)
                        dve.tensor_scalar(y, y, 0.5, None, ALU.mult).then_inc(st.tell(m3, c + 1), 1)
                        dve.scalar_tensor_tensor(g_at[c], th[2 + c % 2], 1.0, g_at[c], ALU.add, ALU.mult).then_inc(st.step(), 1)
                        dve.wait_ge(m4.h, m4.at(c + 1))
                        dve.tensor_tensor(h_lo[:, 8 + c, 0:T], y, h_hi[:, 8 + c, 0:T].bitcast(F32), ALU.subtract).then_inc(st.step(), 1)
                        dve.wait_ge(st.sem, st.now)
                        dve.tensor_scalar(ub[c], g_at[c], 0.25, None, ALU.mult).then_inc(st.step(), 1)
                    st.end()
            for c in range(8):
                loaded[c].base += 48
            m1.base += 8
            m2.base += 16
            m3.base += 8
            m4.base += 8
            sg = [xw[:, (16 + q) * T:(17 + q) * T] for q in range(4)]

            with nc.Block() as block:
                @block.sync
                def _(sp):
                    for n in range(4):
                        sp.dma_start(raw[:, n, :], w_glu[n]).then_inc(raw_full[n].h, 16)

                @block.scalar
                def _(act):
                    def split(n):
                        act.wait_ge(raw_full[n].h, raw_full[n].at(16))
                        act.wait_ge(w_used.h, w_used.at(2 * (n - 1)))
                        act.activation(w_hi[:, n % 2, :], raw[:, n, :], ACT.Copy).then_inc(hi_done.h, 1)

                    split(0)
                    for b in range(8):
                        if b % 2 == 0 and b < 6:
                            split(b // 2 + 1)
                        act.wait_ge(w_used.h, w_used.at(b + 1))
                        act.wait_ge(m2.h, m2.at(b - 1))
                        act.activation(sg[b % 2], bank(b % 2), ACT.Tanh, scale=0.5, bias=col("b_glu", b)).then_inc(m1.h, 1)
                        act.wait_ge(m2.h, m2.at(b + 1))
                        act.activation(h_hi[:, b, 0:T], sg[b % 2], ACT.Copy).then_inc(m3.h, 1)

                @block.vector
                def _(dve):
                    st = Steps(dve, vv)

                    def split(n):
                        dve.wait_ge(hi_done.h, hi_done.at(n + 1))
                        dve.tensor_tensor(w_lo[:, n % 2, :], raw[:, n, :], w_hi[:, n % 2, :].bitcast(F32),
                                          ALU.subtract).then_inc(lo_done.h, 1)
                    split(0)
                    for b in range(8):
                        if b % 2 == 0 and b < 6:
                            split(b // 2 + 1)
                        dve.wait_ge(m1.h, m1.at(b + 1))
                        s_ = sg[b % 2]
                        dve.scalar_tensor_tensor(s_, s_, 1.0, y_at[b], ALU.add, ALU.mult).then_inc(st.step(), 1)
                        dve.wait_ge(st.sem, st.now)
                        dve.tensor_tensor(s_, s_, ub[b], ALU.mult).then_inc(st.tell(m2, b + 1), 1)
                        dve.wait_ge(m3.h, m3.at(b + 1))
                        dve.tensor_tensor(h_lo[:, b, 0:T], s_, h_hi[:, b, 0:T].bitcast(F32), ALU.subtract).then_inc(st.step(), 1)
                    st.end()

                @block.tensor
                def _(pe):
                    for b in range(8):
                        n = b // 2
                        pe.wait_ge(lo_done.h, lo_done.at(n + 1))
                        pe.wait_ge(m1.h, m1.at(b - 1))
                        for k in range(8):
                            o = (b % 2) * 1024 + k * P
                            wh, wl = w_hi[:, n % 2, o:o + P], w_lo[:, n % 2, o:o + P]
                            pe.matmul(bank(b % 2), wh, h_hi[:, 8 + k, 0:T], start=k == 0, stop=False)
                            pe.matmul(bank(b % 2), wh, h_lo[:, 8 + k, 0:T], start=False, stop=False)
                            ins = pe.matmul(bank(b % 2), wl, h_hi[:, 8 + k, 0:T], start=False, stop=k == 7)
                        ins.then_inc(w_used.h, 1)
            for r in raw_full:
                r.base += 16
            hi_done.base += 4
            lo_done.base += 4
            w_used.base += 8
            m1.base += 8
            m2.base += 8
            m3.base += 8

        def attention(heads, group, units, nkeys, qcols, q_src, k_src, v_src, g_src, chunk0, mixed=False):
            nch = nkeys // P
            at = [0]

            def take(size):
                at[0] += size
                return xw[:, at[0] - size:at[0]]
            v_t, g_sb, th, res = take(nkeys), take(qcols), take(qcols), take(qcols)
            q_sb = [take(qcols), wide[:, 0:qcols]]
            k_sb = [take(nkeys), wide[:, W:W + nkeys]]
            diag = wide[:, 2 * W:2 * W + qcols]
            v_sb = take(nkeys).rearrange("p (c d) -> p c d", d=P)
            p_sb = [take(nkeys) for _ in range(2)]
            pt = take(nch * qcols).rearrange("p (c q) -> p c q", c=nch)
            mix_sb = take(qcols) if mixed else None
            s_ps, t_ps, o_ps = [psum[0], psum[1]], psum[2], psum[3]
            nu = len(units)
            total = nu * heads
            mx, nm, sm, rs = ([stat[:, 4 * q + z:4 * q + z + 1] for q in range(2)] for z in range(4))
            scale = float(P) ** -0.5
            nkv = heads // group
            cuts = [(0, T)] + ([(T, W)] if qcols > T else [])
            with nc.Block() as block:
                @block.sync
                def _(sp):
                    for i in range(heads):
                        kv = i // group
                        if i > 1:
                            sp.wait_ge(s_ready.h, s_ready.at(nu * (i - 1)))
                        sp.dma_start(q_sb[i % 2], q_src(i)).then_inc(loaded[i % 2].h, 16)
                        if i % group == 0:
                            if kv > 1:
                                sp.wait_ge(s_ready.h, s_ready.at(nu * group * (kv - 1)))
                            sp.dma_start(k_sb[kv % 2], k_src(kv)).then_inc(loaded[2 + kv % 2].h, 16)
                            sp.wait_ge(m3.h, m3.at(kv))
                            sp.dma_start(v_t, v_src(kv)).then_inc(loaded[4].h, 16)
                        sp.wait_ge(m2.h, m2.at(i))
                        sp.dma_start(g_sb, g_src(i)).then_inc(loaded[5].h, 16)
                        if mixed:
                            sp.wait_ge(mixd_lo.h, mixd_lo.at(i))
                            sp.dma_start(mix_sb, mixd[i][:, 0:qcols]).then_inc(mixd_in.h, 16)

                @block.tensor
                def _(pe):
                    def values(kv):
                        pe.wait_ge(loaded[4].h, loaded[4].at(16 * (kv + 1)))
                        pe.wait_ge(sums_read.h, sums_read.at(kv * group))
                        for c in range(nch):
                            ins = pe.transpose(t_ps[:, c * P:(c + 1) * P], v_t[:, c * P:(c + 1) * P], ident[:])
                        ins.then_inc(m3.h, 1)

                    def scores(g):
                        i, u_ = divmod(g, nu)
                        kv = i // group
                        q0, k0, nk = units[u_]
                        if u_ == 0:
                            pe.wait_ge(loaded[i % 2].h, loaded[i % 2].at(16 * (i // 2 + 1)))
                            pe.wait_ge(loaded[2 + kv % 2].h, loaded[2 + kv % 2].at(16 * (kv // 2 + 1)))
                        pe.wait_ge(exp_done.h, exp_done.at(g - 1))
                        for a in range(0, nk, T):
                            b = min(nk, a + T)
                            ins = pe.matmul(s_ps[g % 2][:, a:b], q_sb[i % 2][:, q0:q0 + P], k_sb[kv % 2][:, k0 + a:k0 + b],
                                            start=True, stop=True)
                        ins.then_inc(s_ready.h, 1)

                    scores(0)
                    scores(1)
                    values(0)
                    for i in range(heads):
                        kv = i // group
                        pe.wait_ge(m4.h, m4.at(kv + 1))
                        pe.wait_ge(sums_read.h, sums_read.at(i))
                        for u_ in range(nu):
                            g = nu * i + u_
                            nk = units[u_][2]
                            pe.wait_ge(exp_done.h, exp_done.at(g + 1))
                            pe.wait_ge(t_out.h, t_out.at(g))
                            for c in range(nk // P):
                                ins = pe.transpose(t_ps[:, c * P:(c + 1) * P], p_sb[g % 2][:, c * P:(c + 1) * P], ident[:])
                            ins.then_inc(t_ready.h, 1)
                            if g + 2 < total:
                                scores(g + 2)
                        pe.wait_ge(p_ready.h, p_ready.at(nu * (i + 1)))
                        pe.wait_ge(t_out.h, t_out.at(nu * (i + 1)))
                        for a, b in cuts:
                            ins = pe.matmul(t_ps[:, a:b], ones[:], diag[:, a:b], start=True, stop=True)
                        ins.then_inc(row_sums.h, 1)
                        pe.wait_ge(m5.h, m5.at(i))
                        for c in range(nch):
                            ins = pe.matmul(o_ps[:, 0:T], v_sb[:, c, :], pt[:, c, 0:T], start=c == 0, stop=c == nch - 1)
                        if qcols > T:
                            for c in range(nch - 2, nch):
                                ins = pe.matmul(o_ps[:, T:W], v_sb[:, c, :], pt[:, c, T:W], start=c == nch - 2, stop=c == nch - 1)
                        ins.then_inc(o_ready.h, 1)
                        if (i + 1) % group == 0 and i + 1 < heads:
                            values(kv + 1)

                @block.gpsimd
                def _(pool):
                    for g in range(total):
                        u_ = g % nu
                        pool.wait_ge(inverted.h, inverted.at(g + 1))
                        pool.wait_ge(row_sums.h, row_sums.at(g // nu))
                        q0 = units[u_][0]
                        pool.tensor_tensor(diag[:, q0:q0 + P], ident[:], rs[g % 2].to_broadcast([P, P]), ALU.mult).then_inc(p_ready.h, 1)

                @block.scalar
                def _(act):
                    def v_out(kv):
                        act.wait_ge(m3.h, m3.at(kv + 1))
                        act.wait_ge(o_ready.h, o_ready.at(kv * group))
                        act.activation(v_sb.rearrange("p c d -> p (c d)"), t_ps[:, 0:nkeys], ACT.Copy).then_inc(m4.h, 1)

                    def exp(g):
                        nk = units[g % nu][2]
                        act.wait_ge(neg_max.h, neg_max.at(g + 1))
                        act.wait_ge(t_ready.h, t_ready.at(g - 1))
                        act.wait_ge(inverted.h, inverted.at(g - 1))
                        act.activation(p_sb[g % 2][:, 0:nk], s_ps[g % 2][:, 0:nk], ACT.Exp, bias=nm[g % 2],
                                       scale=scale, accum_out=sm[g % 2]).then_inc(exp_done.h, 1)
                    exp(0)
                    exp(1)
                    v_out(0)
                    for i in range(heads):
                        for u_ in range(nu):
                            g = nu * i + u_
                            if g + 2 < total:
                                exp(g + 2)
                        act.wait_ge(loaded[5].h, loaded[5].at(16 * (i + 1)))
                        act.wait_ge(m5.h, m5.at(i))
                        act.activation(th, g_sb, ACT.Tanh, scale=0.5).then_inc(m1.h, 1)
                        if mixed:
                            act.wait_ge(mixd_in.h, mixd_in.at(16 * (i + 1)))
                            act.activation(h_hi[:, 8 + i, 0:qcols], mix_sb, ACT.Copy).then_inc(mixd_hi.h, 1)
                        if (i + 1) % group == 0 and i + 1 < heads:
                            v_out(i // group + 1)
                        act.wait_ge(m5.h, m5.at(i + 1))
                        act.activation(h_hi[:, chunk0 + i, 0:qcols], res, ACT.Copy).then_inc(m6.h, 1)

                @block.vector
                def _(dve):
                    st = Steps(dve, vv)

                    def peak(g):
                        nk = units[g % nu][2]
                        dve.wait_ge(s_ready.h, s_ready.at(g + 1))
                        dve.tensor_reduce(mx[g % 2], s_ps[g % 2][:, 0:nk], AX.X, ALU.max).then_inc(st.step(), 1)
                        dve.wait_ge(st.sem, st.now)
                        dve.tensor_scalar(nm[g % 2], mx[g % 2], -scale, None, ALU.mult).then_inc(st.tell(neg_max, g + 1), 1)

                    def low(i):
                        dve.wait_ge(m6.h, m6.at(i + 1))
                        dve.tensor_tensor(h_lo[:, chunk0 + i, 0:qcols], res, h_hi[:, chunk0 + i, 0:qcols].bitcast(F32),
                                          ALU.subtract).then_inc(st.step(), 1)
                        dve.wait_ge(st.sem, st.now)
                    peak(0)
                    peak(1)
                    for i in range(heads):
                        for u_ in range(nu):
                            g = nu * i + u_
                            q0, k0, nk = units[u_]
                            dve.wait_ge(exp_done.h, exp_done.at(g + 1))
                            dve.wait_ge(p_ready.h, p_ready.at(g - 1))
                            dve.reciprocal(rs[g % 2], sm[g % 2]).then_inc(inverted.h, 1)
                            dve.wait_ge(t_ready.h, t_ready.at(g + 1))
                            if u_ == 0:
                                dve.wait_ge(o_ready.h, o_ready.at(i))
                            dve.tensor_copy(pt[:, k0 // P:(k0 + nk) // P, q0:q0 + P],
                                            t_ps[:, 0:nk].rearrange("p (c q) -> p c q", q=P)).then_inc(t_out.h, 1)
                            if g + 2 < total:
                                peak(g + 2)
                        dve.wait_ge(m1.h, m1.at(i + 1))
                        dve.scalar_tensor_tensor(th, th, 1.0, g_sb, ALU.add, ALU.mult).then_inc(st.tell(m2, i + 1), 1)
                        dve.wait_ge(st.sem, st.now)
                        dve.wait_ge(row_sums.h, row_sums.at(i + 1))
                        dve.tensor_tensor(th, th, t_ps[:, 0:qcols], ALU.mult).then_inc(st.tell(sums_read, i + 1), 1)
                        if mixed:
                            dve.wait_ge(mixd_hi.h, mixd_hi.at(i + 1))
                            dve.tensor_tensor(h_lo[:, 8 + i, 0:qcols], mix_sb, h_hi[:, 8 + i, 0:qcols].bitcast(F32),
                                              ALU.subtract).then_inc(mixd_lo.h, 1)
                        if i:
                            low(i - 1)
                        dve.wait_ge(st.sem, st.now)
                        dve.wait_ge(o_ready.h, o_ready.at(i + 1))
                        dve.scalar_tensor_tensor(res, o_ps[:, 0:qcols], 0.5, th, ALU.mult, ALU.mult).then_inc(m5.h, 1)
                    low(heads - 1)
                    st.end()
            loaded[0].base += 16 * ((heads + 1) // 2)
            loaded[1].base += 16 * (heads // 2)
            loaded[2].base += 16 * ((nkv + 1) // 2)
            loaded[3].base += 16 * (nkv // 2)
            loaded[4].base += 16 * nkv
            loaded[5].base += 16 * heads
            for s in (s_ready, neg_max, exp_done, inverted, p_ready, t_ready, t_out):
                s.base += total
            for s in (o_ready, row_sums, sums_read, m1, m2, m5, m6):
                s.base += heads
            m3.base += nkv
            m4.base += nkv
            if mixed:
                mixd_in.base += 16 * heads
                mixd_hi.base += heads
                mixd_lo.base += heads

        def rope_tables():
            cos1, sin1 = raw1[:, 0:T], raw1[:, T:2 * T]
            ang, k_, p_i = (xw[:, q * T:(q + 1) * T] for q in range(3))
            two_pi = 2.0 * math.pi
            c1, c2 = 6.28125, 0.0019350051879882812
            c3 = two_pi - c1 - c2
            magic = 12582912.0
            with nc.Block() as block:
                @block.sync
                def _(sp):
                    sp.dma_start(p_i.bitcast(I32), pos.to_broadcast([P, T])).then_inc(m1.h, 16)

                @block.vector
                def _(dve):
                    st = Steps(dve, vv)
                    dve.wait_ge(m1.h, m1.at(16))
                    dve.tensor_copy(ang, p_i.bitcast(I32)).then_inc(st.step(), 1)
                    dve.wait_ge(st.sem, st.now)
                    dve.tensor_scalar(ang, ang, col("inv_freq"), None, ALU.mult).then_inc(st.step(), 1)
                    for dst, quarter in ((sin1, 0.0), (cos1, 0.25)):
                        dve.wait_ge(st.sem, st.now)
                        dve.tensor_scalar(k_, ang, 1.0 / two_pi, quarter, ALU.mult, ALU.add).then_inc(st.step(), 1)
                        for x in (magic, -magic):
                            dve.wait_ge(st.sem, st.now)
                            dve.tensor_scalar(k_, k_, x, None, ALU.add).then_inc(st.step(), 1)
                        src = ang
                        for c in (c1, c2, c3):
                            dve.wait_ge(st.sem, st.now)
                            dve.scalar_tensor_tensor(dst, k_, -c, src, ALU.mult, ALU.add).then_inc(st.step(), 1)
                            src = dst
                        if quarter:
                            dve.wait_ge(st.sem, st.now)
                            dve.tensor_scalar(dst, dst, math.pi / 2, None, ALU.add).then_inc(st.step(), 1)
                        dve.wait_ge(st.sem, st.now)
                        dve.tensor_scalar(dst, dst, 3.1415925, -3.1415925, ALU.min, ALU.max).then_inc(st.tell(m2, 2 if quarter else 1), 1)
                    st.end()

                @block.scalar
                def _(act):
                    act.wait_ge(m2.h, m2.at(1))
                    act.activation(sin1, sin1, ACT.Sin)
                    act.wait_ge(m2.h, m2.at(2))
                    act.activation(cos1, cos1, ACT.Sin)
            m1.base += 16
            m2.base += 2

        def diff_attention():
            cos1, sin1 = raw1[:, 0:T], raw1[:, T:2 * T]
            mask_sb = raw1[:, 2 * T:2 * T + P]
            o_sb = [raw1[:, (3 + h) * T:(4 + h) * T] for h in range(4)]
            at = [0]

            def take(size):
                at[0] += size
                return xw[:, at[0] - size:at[0]]
            q_sb, k_sb, v_t, qr, kr, r1, r2 = (take(T) for _ in range(7))
            v_sb = take(T).rearrange("p (c d) -> p c d", d=P)
            p_sb = [[take(T) for _ in range(2)] for _ in range(2)]
            w_sb = [take(T) for _ in range(2)]
            wt = take(TB * T).rearrange("p (c q) -> p c q", c=TB)
            s_ps = [[bank(0), bank(1)], [bank(2), bank(3)]]
            t_ps, o_ps, r_ps, v_ps = bank(4), bank(5), bank(6), bank(7)
            scale = 64.0 ** -0.5
            H = 4

            def st4(q, c, j):
                o = 8 * q + 4 * c + j
                return stat[:, o:o + 1]
            with nc.Block() as block:
                @block.sync
                def _(sp):
                    sp.dma_start(mask_sb, const[:, 2 * P:3 * P]).then_inc(loaded[3].h, 16)

                    def body(i):
                        sp.wait_ge(m1.h, m1.at(2 * i))
                        sp.dma_start(q_sb, row(proj, i + 16)).then_inc(loaded[0].h, 16)
                        sp.dma_start(k_sb, row(proj, i + 20)).then_inc(loaded[0].h, 16)
                        sp.wait_ge(m3.h, m3.at(i))
                        sp.dma_start(v_t, row(proj, i + 24)).then_inc(loaded[1].h, 16)
                    Steps(sp, vp).loop(H, body)

                @block.tensor
                def _(pe):
                    def scores(i, b):
                        pe.wait_ge(exp_done.h, exp_done.at(2 * (4 * i + b) - 2))
                        for c in range(2):
                            ins = pe.matmul(s_ps[b % 2][c][:, 0:(b + 1) * P], qr[64 * c:64 * c + 64, b * P:(b + 1) * P],
                                            kr[64 * c:64 * c + 64, 0:(b + 1) * P], start=True, stop=True)
                        ins.then_inc(s_ready.h, 1)

                    def body(i):
                        pe.wait_ge(loaded[0].h, loaded[0].at(32 * (i + 1)))
                        pe.wait_ge(m2.h, m2.at(2 * i))
                        pe.matmul(r_ps, rot[:], q_sb, start=True, stop=True).then_inc(rms_ready.h, 1)
                        pe.wait_ge(m2.h, m2.at(2 * i + 1))
                        pe.matmul(r_ps, rot[:], k_sb, start=True, stop=True).then_inc(rms_ready.h, 1)
                        pe.wait_ge(loaded[1].h, loaded[1].at(16 * (i + 1)))
                        pe.wait_ge(m4.h, m4.at(i))
                        for c in range(TB):
                            ins = pe.transpose(v_ps[:, c * P:(c + 1) * P], v_t[:, c * P:(c + 1) * P], ident[:])
                        ins.then_inc(m3.h, 1)
                        pe.wait_ge(m1.h, m1.at(2 * i + 2))
                        scores(i, 0)
                        for b in range(TB):
                            if b + 1 < TB:
                                scores(i, b + 1)
                            pe.wait_ge(p_ready.h, p_ready.at(4 * i + b + 1))
                            pe.wait_ge(t_out.h, t_out.at(4 * i + b))
                            for c in range(b + 1):
                                ins = pe.transpose(t_ps[:, c * P:(c + 1) * P], w_sb[b % 2][:, c * P:(c + 1) * P], ident[:])
                            ins.then_inc(t_ready.h, 1)
                        pe.wait_ge(t_out.h, t_out.at(4 * i + 4))
                        pe.wait_ge(m4.h, m4.at(i + 1))
                        pe.wait_ge(o_read.h, o_read.at(i))
                        for c in range(TB):
                            ins = pe.matmul(o_ps[:, c * P:T], v_sb[:, c, :], wt[:, c, c * P:T], start=c == 0, stop=c == TB - 1)
                        ins.then_inc(o_ready.h, 1)
                    Steps(pe, vp).loop(H, body)

                @block.scalar
                def _(act):
                    def turned(i, b):
                        act.wait_ge(t_ready.h, t_ready.at(4 * i + b + 1))
                        if b == 0:
                            act.wait_ge(o_ready.h, o_ready.at(i))
                        act.activation(wt[:, 0:b + 1, b * P:(b + 1) * P],
                                       t_ps[:, 0:(b + 1) * P].rearrange("p (c q) -> p c q", q=P), ACT.Copy).then_inc(t_out.h, 1)

                    def body(i):
                        act.wait_ge(m3.h, m3.at(i + 1))
                        act.wait_ge(o_ready.h, o_ready.at(i))
                        act.activation(v_sb.rearrange("p c d -> p (c d)"), v_ps, ACT.Copy).then_inc(m4.h, 1)
                        for b in range(TB):
                            g = 4 * i + b
                            nk = (b + 1) * P
                            act.wait_ge(neg_max.h, neg_max.at(g + 1))
                            act.wait_ge(p_ready.h, p_ready.at(g - 1))
                            for c in range(2):
                                act.activation(p_sb[b % 2][c][:, 0:nk], s_ps[b % 2][c][:, 0:nk], ACT.Exp, bias=st4(b % 2, c, 1),
                                               scale=scale, accum_out=st4(b % 2, c, 2)).then_inc(exp_done.h, 1)
                            if b:
                                turned(i, b - 1)
                        turned(i, TB - 1)
                        act.wait_ge(o_ready.h, o_ready.at(i + 1))
                        dst = raw1[:, bass.ds(i * T + 3 * T, T)] if not isinstance(i, int) else o_sb[i]
                        act.activation(dst, o_ps, ACT.Copy).then_inc(o_read.h, 1)
                    Steps(act, va).loop(H, body)

                @block.vector
                def _(dve):
                    st = Steps(dve, vv)

                    def peak(i, b):
                        nk = (b + 1) * P
                        dve.wait_ge(s_ready.h, s_ready.at(4 * i + b + 1))
                        for c in range(2):
                            d = s_ps[b % 2][c][:, nk - P:nk]
                            dve.tensor_tensor(d, d, mask_sb, ALU.add).then_inc(st.step(), 1)
                        dve.wait_ge(st.sem, st.now)
                        for c in range(2):
                            dve.tensor_reduce(st4(b % 2, c, 0), s_ps[b % 2][c][:, 0:nk], AX.X, ALU.max).then_inc(st.step(), 1)
                        dve.wait_ge(st.sem, st.now)
                        dve.tensor_scalar(st4(b % 2, 0, 1), st4(b % 2, 0, 0), -scale, None, ALU.mult).then_inc(st.step(), 1)
                        dve.tensor_scalar(st4(b % 2, 1, 1), st4(b % 2, 1, 0), -scale, None, ALU.mult).then_inc(st.tell(neg_max, 4 * i + b + 1), 1)

                    def body(i):
                        for n, (src, dst) in enumerate(((q_sb, qr), (k_sb, kr))):
                            dve.wait_ge(loaded[0].h, loaded[0].at(32 * (i + 1)))
                            dve.wait_ge(s_ready.h, s_ready.at(4 * i))
                            dve.wait_ge(st.sem, st.now)
                            dve.tensor_tensor(r1, src, cos1, ALU.mult).then_inc(st.step(), 1)
                            dve.wait_ge(rms_ready.h, rms_ready.at(2 * i + n + 1))
                            dve.tensor_tensor(r2, r_ps, sin1, ALU.mult).then_inc(st.tell(m2, 2 * i + n + 1), 1)
                            dve.wait_ge(st.sem, st.now)
                            dve.tensor_tensor(dst, r1, r2, ALU.add).then_inc(st.tell(m1, 2 * i + n + 1), 1)
                        peak(i, 0)
                        for b in range(TB):
                            g = 4 * i + b
                            nk = (b + 1) * P
                            if b + 1 < TB:
                                peak(i, b + 1)
                            dve.wait_ge(exp_done.h, exp_done.at(2 * g + 2))
                            p0, p1 = (x[:, 0:nk] for x in p_sb[b % 2])
                            for c in range(2):
                                dve.reciprocal(st4(b % 2, c, 3), st4(b % 2, c, 2)).then_inc(st.step(), 1)
                            dve.wait_ge(st.sem, st.now)
                            dve.tensor_scalar(p1, p1, st4(b % 2, 1, 3), lam[:, 6:7], ALU.mult, ALU.mult).then_inc(st.step(), 1)
                            dve.wait_ge(st.sem, st.now)
                            dve.wait_ge(t_ready.h, t_ready.at(g - 1))
                            dve.scalar_tensor_tensor(w_sb[b % 2][:, 0:nk], p0, st4(b % 2, 0, 3), p1, ALU.mult, ALU.subtract).then_inc(st.tell(p_ready, g + 1), 1)
                    dve.wait_ge(loaded[3].h, loaded[3].at(16))
                    st.loop(H, body)
                    st.end()
            for s, v in ((loaded[0], 128), (loaded[1], 64), (loaded[3], 16), (m1, 8), (m2, 8), (m3, 4), (m4, 4),
                         (rms_ready, 8), (s_ready, 16), (neg_max, 16), (exp_done, 32), (p_ready, 16), (t_ready, 16),
                         (t_out, 16), (o_ready, 4), (o_read, 4)):
                s.base += v
            g_sb, th, sq, rt, res = ([xw[:, (5 * q + z) * T:(5 * q + z + 1) * T] for q in range(4)] for z in range(5))
            with nc.Block() as block:
                @block.sync
                def _(sp):
                    for h in range(H):
                        sp.dma_start(g_sb[h], proj[28 + h]).then_inc(loaded[0].h, 16)

                @block.scalar
                def _(act):
                    for h in range(H):
                        act.activation(sq[h], o_sb[h], ACT.Square).then_inc(m1.h, 1)
                    for h in range(H):
                        act.wait_ge(m2.h, m2.at(h + 1))
                        act.activation(rt[h], bank(h), ACT.Sqrt, bias=lam[:, 7:8], scale=1.0 / P).then_inc(m3.h, 1)
                    act.wait_ge(loaded[0].h, loaded[0].at(64))
                    for h in range(H):
                        act.activation(th[h], g_sb[h], ACT.Tanh, scale=0.5).then_inc(m4.h, 1)
                    for h in range(H):
                        act.wait_ge(m5.h, m5.at(h + 1))
                        act.activation(h_hi[:, 8 + h, 0:T], res[h], ACT.Copy).then_inc(m6.h, 1)

                @block.tensor
                def _(pe):
                    for h in range(H):
                        pe.wait_ge(m1.h, m1.at(h + 1))
                        pe.matmul(bank(h), ones[:], sq[h], start=True, stop=True).then_inc(m2.h, 1)

                @block.vector
                def _(dve):
                    st = Steps(dve, vv)
                    for h in range(H):
                        dve.wait_ge(m3.h, m3.at(h + 1))
                        dve.reciprocal(rt[h], rt[h]).then_inc(st.step(), 1)
                        dve.wait_ge(st.sem, st.now)
                        dve.scalar_tensor_tensor(o_sb[h], o_sb[h], col("subln"), rt[h], ALU.mult, ALU.mult).then_inc(st.step(), 1)
                        dve.wait_ge(m4.h, m4.at(h + 1))
                        dve.scalar_tensor_tensor(th[h], th[h], 1.0, g_sb[h], ALU.add, ALU.mult).then_inc(st.step(), 1)
                        dve.wait_ge(st.sem, st.now)
                        dve.tensor_tensor(res[h], o_sb[h], th[h], ALU.mult).then_inc(st.tell(m5, h + 1), 1)
                        dve.wait_ge(m6.h, m6.at(h + 1))
                        dve.tensor_tensor(h_lo[:, 8 + h, 0:T], res[h], h_hi[:, 8 + h, 0:T].bitcast(F32), ALU.subtract).then_inc(st.step(), 1)
                    st.end()
            loaded[0].base += 64
            for m in (m1, m2, m3, m4, m5, m6):
                m.base += H

        def out_projection(weights, base, segs, gate_layer):
            a0, a1 = segs[0][0], segs[-1][1]

            def xrow(n):
                return (lambda a, b: xw[:, bass.ds(n * W + a, b - a)]) if not isinstance(n, int) else \
                    (lambda a, b: xk[:, n, a:b])

            def act_out(st, n, accs):
                st.eng.wait_ge(sq_ready.h, sq_ready.at(n + 1))
                st.eng.wait_ge(sq_summed.h, sq_summed.at(n))
                st.eng.activation(tmp[:, a0:a1], xrow(n)(a0, a1), ACT.Square).then_inc(sum_ready.h, 1)

            def vec_out(st, n, accs):
                dve = st.eng
                dve.wait_ge(w_used.h, w_used.at(n + 1))
                if gate_layer is not None and isinstance(n, int):
                    dve.wait_ge(resid_in.h, resid_in.at(64))
                for q, (a, b) in enumerate(segs):
                    x = xrow(n)(a, b)
                    if gate_layer is None:
                        ins = dve.tensor_copy(x, accs[q])
                    else:
                        if isinstance(n, int):
                            g = mods[:, gate_layer, 32 + n, q:q + 1]
                        else:
                            g = mods[:].rearrange("p l k s -> p (l k s)")[:, bass.ds(n * 2 + gate_layer * 96 + 64 + q, 1)]
                        ins = dve.scalar_tensor_tensor(x, accs[q], g, x, ALU.mult, ALU.add)
                    if q < len(segs) - 1:
                        ins.then_inc(st.step(), 1)
                        dve.wait_ge(st.sem, st.now)
                    else:
                        ins.then_inc(st.tell(acc_free_v, n + 1), 1)
                        dve.wait_ge(st.sem, st.now)
                dve.tensor_scalar(stat[:, 20:21], lam[:, 7:8], 1.0, None, ALU.mult).then_inc(st.tell(sq_ready, n + 1), 1)
                dve.wait_ge(sum_ready.h, sum_ready.at(n + 1))
                dve.wait_ge(st.sem, st.now)
                dve.tensor_tensor(acc_sq[:, a0:a1], acc_sq[:, a0:a1], tmp[:, a0:a1], ALU.add).then_inc(st.tell(sq_summed, n + 1), 1)

            with nc.Block() as block:
                @block.vector
                def _(dve):
                    dve.memset(acc_sq[:, a0:a1], 0.0)

            def reload(sp):
                for q in range(4):
                    sp.dma_start(xk[:, 4 * q:4 * q + 4, :], resid[4 * q:4 * q + 4].rearrange("k p n -> p k n")).then_inc(resid_in.h, 16)
            keeps = gate_layer is not None and gate_layer < LAYERS - 1
            linear(4, lambda n: row(weights, n + base), KC, 0, segs, act_out=act_out, vec_out=vec_out,
                   beside=None if gate_layer is None else reload,
                   keep=(lambda n: (row(resid, n), xrow(n)(0, W))) if keeps else None)
            if gate_layer is not None:
                resid_in.base += 64
            if keeps:
                resid_out.base += 16 * KC
            for s in (sq_ready, sq_summed, sum_ready):
                s.base += 16

        def between_blocks():
            xin = [raw1[:, q * 4 * T:(q + 1) * 4 * T] for q in range(4)]
            with nc.Block() as block:
                @block.sync
                def _(sp):
                    for q in range(4):
                        sp.dma_start(xin[q].rearrange("p (k n) -> p k n", k=4), x_in[:, 4 * q:4 * q + 4, :]).then_inc(loaded[q].h, 16)
                    for q in range(4):
                        sp.dma_start(xk[:, 4 * q:4 * q + 4, T:W], ctx_in[:, 4 * q:4 * q + 4, :]).then_inc(loaded[4].h, 16)
                    sp.wait_ge(loaded[4].h, loaded[4].at(64))
                    for q in range(4):
                        sp.wait_ge(m1.h, m1.at(4 * q + 4))
                        sp.dma_start(resid[4 * q:4 * q + 4].rearrange("k p n -> p k n"), xk[:, 4 * q:4 * q + 4, :]).then_inc(m2.h, 16)
                    sp.wait_ge(m2.h, m2.at(64))

                @block.tensor
                def _(pe):
                    pe.matmul(bank(0), ones[:], acc_sq[:, 0:T], start=True, stop=True).then_inc(m3.h, 1)

                @block.scalar
                def _(act):
                    act.wait_ge(m3.h, m3.at(1))
                    act.activation(tmp[:, 0:T], bank(0), ACT.Sqrt, bias=lam[:, 7:8], scale=1.0 / D).then_inc(m4.h, 1)

                @block.vector
                def _(dve):
                    st = Steps(dve, vv)
                    dve.wait_ge(m4.h, m4.at(1))
                    dve.reciprocal(rstd[:, 0:T], tmp[:, 0:T]).then_inc(st.step(), 1)
                    dve.wait_ge(st.sem, st.now)
                    for k in range(KC):
                        x = xk[:, k, 0:T]
                        dve.scalar_tensor_tensor(x, x, col("norm_post", k), rstd[:, 0:T], ALU.mult, ALU.mult).then_inc(st.step(), 1)
                        dve.wait_ge(st.sem, st.now)
                        dve.wait_ge(loaded[k // 4].h, loaded[k // 4].at(16))
                        dve.tensor_tensor(x, x, xin[k // 4][:, (k % 4) * T:(k % 4 + 1) * T], ALU.add).then_inc(st.tell(m1, k + 1), 1)
                    st.end()
            for q in range(4):
                loaded[q].base += 16
            loaded[4].base += 64
            m1.base += KC
            m2.base += 64
            m3.base += 1
            m4.base += 1

        def projections(l):
            both, lat = [(0, T), (T, W)], [(0, T)]
            if l == LAYERS - 1:
                width = T
                parts = [(2, 0, lat, None), (1, 8, both, None), (1, 12, lat, None), (3, 16, lat, "qk"), (2, 28, lat, "mix")]
            else:
                width = W
                parts = [(4, 0, both, None), (3, 16, both, "qk"), (2, 28, both, "mix")]
            units = HEADS2 + KV2
            both_w = width > T
            stage = [xw[:, q * W:(q + 1) * W] for q in range(2)]
            at = [2 * W]

            def take(size):
                at[0] += size
                return xw[:, at[0] - size:at[0]]
            cn = take(D).rearrange("p (m n) -> p m n", m=4)
            sn = take(D).rearrange("p (m n) -> p m n", m=4)
            cs_fw = take(8 * P)
            pw = take(4 * P).rearrange("p (g d) -> p g d", g=4)
            side0 = at[0]
            q_sb = [take(W) for _ in range(4)]
            sq, root, turned = take(W), take(W), take(T)
            qn, cos2, sin2 = wide[:, 0:W], wide[:, W:W + T], wide[:, W + T:W + 2 * T]
            at[0] = side0
            pad = 800
            tok = [(8, 0, T)] + ([(536, T, W)] if both_w else [])
            sums = [take(pad) for _ in range(2)]
            y = take(6 * 256).rearrange("p (m c) -> p m c", m=6)
            up, uf = take(pad), take(W)
            cnt, f_gate, f_th = (wide[:, q * W:(q + 1) * W] for q in range(3))
            p_gate = cnt
            p_th = [sums[g % 2] for g in range(4)]
            pl = [sums[1 - g % 2] for g in range(4)]
            stat_ps, rot_ps = psum[2], bank(6)
            pool_ps, f_lat, f_ctx = psum[2], bank(7), bank(6)[:, 0:CT]
            nch = width // P
            f_scale = [0.5 / math.sqrt(T * P), 0.5 / math.sqrt(CT * P)]

            def accs(n, segs):
                return [bank(2 * n + q)[:, 0:b - a] for q, (a, b) in enumerate(segs)]

            def turns(st, iters, body, kind, missing=0):
                if kind == "mix":
                    for i in range(iters):
                        body(i)
                else:
                    st.loop(iters, body, missing=missing)

            with nc.Block() as block:
                @block.sync
                def _(sp):
                    st = Steps(sp, vp)
                    before = None
                    for iters, n0, segs, kind in parts:
                        def body(i):
                            for j in range(4):
                                n = n0 + 4 * i + j
                                sp.wait_ge(hi_done.h, hi_done.at(n - 3))
                                sp.wait_ge(lo_done.h, lo_done.at(n - 3))
                                sp.dma_start(raw[:, j, :], row(w_in2, n + l * IN2)).then_inc(raw_full[j].h, 16)
                                if not (n0 == 0 and first(i) and j < 2):
                                    w_ = (before if first(i) and j < 2 else segs)[-1][1]
                                    sp.wait_ge(staged.h, staged.at(n - 1))
                                    sp.dma_start(row(proj2, n - 2)[:, 0:w_], stage[j % 2][:, 0:w_]).then_inc(stored[j % 2].h, 16)
                                if kind == "qk":
                                    qk_turn(i, j, 4 * i + j)
                                if kind == "mix":
                                    mix_turn(4 * i + j)

                        def qk_turn(i, j, s):
                            if first(i) and j == 0:
                                sp.wait_ge(stored[0].h, stored[0].at(16 * 6))
                                sp.wait_ge(stored[1].h, stored[1].at(16 * 6))
                                sp.dma_start(cos2, rope2[:, 0:T]).then_inc(rope_in.h, 16)
                                sp.dma_start(sin2, rope2[:, T:2 * T]).then_inc(rope_in.h, 16)
                            sp.wait_ge(q_out[j].h, q_out[j].at(16 * i))
                            sp.dma_start(q_sb[j], row(proj2, s)).then_inc(q_in[j].h, 16)
                            if not (first(i) and j < 3):
                                sp.wait_ge(q_done.h, q_done.at(s - 2))
                                sp.dma_start(row(proj2, s - 3), q_sb[(j + 1) % 4]).then_inc(q_out[(j + 1) % 4].h, 16)
                            if first(i) and j == 3:
                                sp.dma_start(cn.rearrange("p m n -> p (m n)"), cn_sn[:, 0:D]).then_inc(mix_in.h, 16)
                                sp.dma_start(sn.rearrange("p m n -> p (m n)"), cn_sn[:, D:2 * D]).then_inc(mix_in.h, 16)
                                sp.dma_start(cs_fw, four_m[l]).then_inc(mix_in.h, 16)
                                sp.dma_start(pw, pool_w[l]).then_inc(mix_in.h, 16)

                        def load_pool(g):
                            sp.wait_ge(stored[g % 2].h, stored[g % 2].at(16 * ((12 + g) // 2 + 1)))
                            sp.wait_ge(pooled.h, pooled.at(g))
                            for b0, t0, t1 in tok:
                                sp.dma_start(up[:, b0:b0 + t1 - t0], proj2[12 + g][:, t0:t1]).then_inc(up_in.h, 16)

                        def load_four(g):
                            sp.wait_ge(stored[g % 2].h, stored[g % 2].at(16 * ((16 + g) // 2 + 1)))
                            sp.wait_ge(chan_done.h, chan_done.at(g))
                            sp.dma_start(uf[:, 0:width], proj2[16 + g][:, 0:width]).then_inc(uf_in.h, 16)

                        def load_pool_gate(g):
                            sp.wait_ge(stored[g % 2].h, stored[g % 2].at(16 * ((20 + g) // 2 + 1)))
                            sp.wait_ge(pooled.h, pooled.at(g + 1))
                            sp.dma_start(p_gate[:, 0:width], proj2[20 + g][:, 0:width]).then_inc(pgate_in.h, 16)

                        def store_mixed(g):
                            sp.wait_ge(pool_out.h, pool_out.at(g + 1))
                            sp.dma_start(mixd[g][:, 0:width], p_th[g][:, 0:width]).then_inc(pool_st.h, 16)
                            sp.wait_ge(four_out.h, four_out.at(g + 1))
                            sp.dma_start(mixd[4 + g][:, 0:width], f_th[:, 0:width]).then_inc(four_st.h, 16)

                        def mix_turn(c):
                            g = c // 2
                            if c == 0:
                                sp.wait_ge(q_done.h, q_done.at(units))
                                sp.dma_start(proj2[units - 1], q_sb[1]).then_inc(q_out[1].h, 16)
                                for q in range(4):
                                    sp.wait_ge(q_out[q].h, q_out[q].at(48 if q < 2 else 32))
                                sp.wait_ge(sums_done.h, sums_done.at(units + 2))
                                sp.wait_ge(qn_done.h, qn_done.at(units + 1))
                                sp.wait_ge(rot_done.h, rot_done.at(units + 1))
                            if c % 2 == 0:
                                if g:
                                    load_pool_gate(g - 1)
                                load_four(g)
                                load_pool(g)
                            else:
                                if g:
                                    store_mixed(g - 1)
                                sp.wait_ge(pool_out.h, pool_out.at(g))
                                sp.dma_start(cnt, invcnt[g:g + 1, :].to_broadcast([P, W])).then_inc(cnt_in.h, 16)
                                sp.wait_ge(stored[g % 2].h, stored[g % 2].at(16 * ((24 + g) // 2 + 1)))
                                sp.wait_ge(four_out.h, four_out.at(g))
                                sp.dma_start(f_gate[:, 0:width], proj2[24 + g][:, 0:width]).then_inc(fgate_in.h, 16)
                        turns(st, iters, body, kind)
                        before = segs
                    load_pool_gate(3)
                    for n in (34, 35):
                        sp.wait_ge(staged.h, staged.at(n + 1))
                        sp.dma_start(proj2[n][:, 0:width], stage[n % 2][:, 0:width]).then_inc(stored[n % 2].h, 16)
                    store_mixed(3)
                    for q in range(2):
                        sp.wait_ge(stored[q].h, stored[q].at(16 * IN2 // 2))
                    sp.wait_ge(pool_st.h, pool_st.at(64))
                    sp.wait_ge(four_st.h, four_st.at(64))

                @block.scalar
                def _(act):
                    st = Steps(act, va)
                    before = None
                    for iters, n0, segs, kind in parts:
                        def read_out(n, par, segs_):
                            act.wait_ge(w_used.h, w_used.at(n + 1))
                            act.wait_ge(stored[par].h, stored[par].at(8 * (n - par)))
                            for a_, (a, b) in zip(accs(par, segs_), segs_):
                                ins = act.activation(stage[par][:, a:b], a_, ACT.Copy)
                            ins.then_inc(staged.h, 1)

                        def body(i):
                            for j in range(4):
                                n = n0 + 4 * i + j
                                act.wait_ge(raw_full[j].h, raw_full[j].at(4 * (n - j) + 16))
                                act.wait_ge(w_used.h, w_used.at(n - 1))
                                act.activation(w_hi[:, j % 2, :], raw[:, j, :], ACT.Copy).then_inc(hi_done.h, 1)
                                if not (n0 == 0 and first(i) and j == 0):
                                    read_out(n - 1, (j - 1) % 2, before if first(i) and j == 0 else segs)
                                if kind == "qk":
                                    qk_turn(i, j, 4 * i + j)
                                if kind == "mix":
                                    mix_turn(4 * i + j)

                        def qk_turn(i, j, s):
                            if not (first(i) and j == 0):
                                act.wait_ge(sums_done.h, sums_done.at(s))
                                act.wait_ge(qn_done.h, qn_done.at(s - 1))
                                act.activation(root, stat_ps[:, 0:W], ACT.Sqrt, bias=lam[:, 7:8], scale=1.0 / P).then_inc(root_done.h, 1)
                            act.wait_ge(q_in[j].h, q_in[j].at(16 * (i + 1)))
                            act.activation(sq, q_sb[j], ACT.Square).then_inc(sq_done.h, 1)

                        def mix_turn(c):
                            if c % 2:
                                g = c // 2
                                act.wait_ge(chan_done.h, chan_done.at(g + 1))
                                act.wait_ge(four_done.h, four_done.at(g))
                                if nch > 4:
                                    act.activation(y[:, 4:6, :], bank(6).rearrange("p (m c) -> p m c", m=2), ACT.Copy)
                                act.activation(y[:, 0:4, :], psum[2][:].rearrange("p (m c) -> p m c", m=4), ACT.Copy).then_inc(y_copied.h, 1)
                            elif c:
                                g = c // 2 - 1
                                act.wait_ge(pgate_in.h, pgate_in.at(16 * (g + 1)))
                                act.wait_ge(pooled.h, pooled.at(g + 1))
                                act.activation(p_th[g][:, 0:width], p_gate[:, 0:width], ACT.Tanh, scale=0.5).then_inc(p_tanh.h, 1)
                                act.wait_ge(fgate_in.h, fgate_in.at(16 * (g + 1)))
                                act.wait_ge(four_st.h, four_st.at(16 * g))
                                act.activation(f_th[:, 0:width], f_gate[:, 0:width], ACT.Tanh, scale=0.5).then_inc(f_tanh.h, 1)
                        turns(st, iters, body, kind)
                        before = segs
                    read_out(IN2 - 1, (IN2 - 1) % 2, before)
                    mix_turn(8)
                    st.end()

                @block.vector
                def _(dve):
                    st = Steps(dve, vv)
                    for iters, n0, segs, kind in parts:
                        def body(i):
                            for j in range(4):
                                n = n0 + 4 * i + j
                                dve.wait_ge(hi_done.h, hi_done.at(n + 1))
                                dve.tensor_tensor(w_lo[:, j % 2, :], raw[:, j, :], w_hi[:, j % 2, :].bitcast(F32),
                                                  ALU.subtract).then_inc(lo_done.h, 1)
                                if kind == "qk":
                                    qk_turn(i, j, 4 * i + j)
                                if kind == "mix":
                                    mix_turn(4 * i + j)

                        def qk_turn(i, j, s):
                            if first(i) and j == 0:
                                dve.wait_ge(rope_in.h, rope_in.at(32))
                            if not (first(i) and j < 2):
                                q = q_sb[(j - 2) % 4]
                                dve.wait_ge(qn_done.h, qn_done.at(s - 1))
                                dve.wait_ge(q_done.h, q_done.at(s - 2))
                                dve.tensor_copy(q[:, T:W], qn[:, T:W]).then_inc(st.step(), 1)
                                dve.tensor_tensor(q[:, 0:T], qn[:, 0:T], cos2, ALU.mult).then_inc(st.step(), 1)
                                dve.wait_ge(rot_done.h, rot_done.at(s - 1))
                                dve.tensor_tensor(turned, rot_ps, sin2, ALU.mult).then_inc(rot_read.h, 1)
                                dve.wait_ge(rot_read.h, rot_read.at(s - 1))
                                dve.tensor_tensor(q[:, 0:T], q[:, 0:T], turned, ALU.add).then_inc(q_done.h, 1)
                            if not (first(i) and j == 0):
                                dve.wait_ge(root_done.h, root_done.at(s))
                                dve.reciprocal(root, root).then_inc(st.step(), 1)
                                dve.wait_ge(st.sem, st.now)
                                dve.wait_ge(rot_done.h, rot_done.at(s - 1))
                                dve.scalar_tensor_tensor(qn, q_sb[(j - 1) % 4], col("qk_gain", s + (10 * l - 1)), root,
                                                         ALU.mult, ALU.mult).then_inc(qn_done.h, 1)

                        def mix_turn(c):
                            if c == 0:
                                dve.wait_ge(qn_done.h, qn_done.at(units + 1))
                                dve.wait_ge(sums_done.h, sums_done.at(units + 2))
                                for q in range(4):
                                    dve.wait_ge(q_out[q].h, q_out[q].at(48 if q < 2 else 32))
                                for a, b in ((0, 8), (8 + T, 536), (536 + CT, pad)):
                                    dve.memset(up[:, a:b], 0.0).then_inc(st.step(), 1)
                                if not both_w:
                                    dve.memset(up[:, 536:536 + CT], 0.0).then_inc(st.step(), 1)
                                dve.wait_ge(st.sem, st.now)
                                dve.wait_ge(mix_in.h, mix_in.at(64))
                            elif c % 2:
                                g = c // 2
                                win = 2 << g
                                dve.wait_ge(up_in.h, up_in.at(16 * len(tok) * (g + 1)))
                                dve.wait_ge(pool_st.h, pool_st.at(16 * g))
                                dve.wait_ge(pool_done.h, pool_done.at(g))
                                cur, n, step, other = up, pad, 1, sums
                                while step < win:
                                    n -= step
                                    dve.wait_ge(st.sem, st.now)
                                    dve.tensor_tensor(other[0][:, 0:n], cur[:, 0:n], cur[:, step:step + n], ALU.add).then_inc(st.step(), 1)
                                    cur = other[0]
                                    other = other[::-1]
                                    step *= 2
                                dve.wait_ge(st.sem, st.now)
                                dve.wait_ge(cnt_in.h, cnt_in.at(16 * (g + 1)))
                                for b0, t0, t1 in tok:
                                    s0 = b0 - win // 2
                                    dve.tensor_tensor(pl[g][:, t0:t1], cur[:, s0:s0 + t1 - t0], cnt[:, t0:t1], ALU.mult).then_inc(st.step(), 1)
                                dve.wait_ge(st.sem, st.now)
                                for q, (b0, t0, t1) in enumerate(tok):
                                    ins = dve.tensor_tensor(pl[g][:, t0:t1], pl[g][:, t0:t1], up[:, b0:b0 + t1 - t0], ALU.subtract)
                                    if q == len(tok) - 1:
                                        ins.then_inc(st.tell(pooled, g + 1), 1)
                                    else:
                                        ins.then_inc(st.step(), 1)
                            else:
                                g = c // 2 - 1
                                pt_, ft_ = p_th[g][:, 0:width], f_th[:, 0:width]
                                dve.wait_ge(p_tanh.h, p_tanh.at(g + 1))
                                dve.scalar_tensor_tensor(pt_, pt_, 1.0, p_gate[:, 0:width], ALU.add, ALU.mult).then_inc(st.step(), 1)
                                dve.wait_ge(st.sem, st.now)
                                dve.wait_ge(pool_done.h, pool_done.at(g + 1))
                                dve.scalar_tensor_tensor(pt_, pool_ps[:, 0:width], col("pool_scale", 4 * l + g), pt_,
                                                         ALU.mult, ALU.mult).then_inc(st.tell(pool_out, g + 1), 1)
                                dve.wait_ge(f_tanh.h, f_tanh.at(g + 1))
                                dve.scalar_tensor_tensor(ft_, ft_, 1.0, f_gate[:, 0:width], ALU.add, ALU.mult).then_inc(st.step(), 1)
                                dve.wait_ge(st.sem, st.now)
                                dve.wait_ge(four_done.h, four_done.at(g + 1))
                                if both_w:
                                    dve.scalar_tensor_tensor(f_th[:, T:W], f_ctx, f_scale[1], f_th[:, T:W], ALU.mult, ALU.mult).then_inc(st.step(), 1)
                                dve.scalar_tensor_tensor(f_th[:, 0:T], f_lat, f_scale[0], f_th[:, 0:T], ALU.mult, ALU.mult).then_inc(st.tell(four_out, g + 1), 1)
                        turns(st, iters, body, kind, 5 if kind == "qk" else 0)
                    mix_turn(8)
                    dve.wait_ge(st.sem, st.now)
                    st.end()

                @block.tensor
                def _(pe):
                    st = Steps(pe, vp)
                    for iters, n0, segs, kind in parts:
                        def body(i):
                            for j in range(4):
                                n = n0 + 4 * i + j
                                a_ = accs(j % 2, segs)
                                pe.wait_ge(lo_done.h, lo_done.at(n + 1))
                                pe.wait_ge(staged.h, staged.at(n - 1))
                                for k in range(KC):
                                    wh = w_hi[:, j % 2, k * P:(k + 1) * P]
                                    wl = w_lo[:, j % 2, k * P:(k + 1) * P]
                                    for q, (a, b) in enumerate(segs):
                                        pe.matmul(a_[q], wh, h_hi[:, k, a:b], start=k == 0, stop=False)
                                        pe.matmul(a_[q], wh, h_lo[:, k, a:b], start=False, stop=False)
                                        ins = pe.matmul(a_[q], wl, h_hi[:, k, a:b], start=False, stop=k == KC - 1)
                                ins.then_inc(w_used.h, 1)
                                if kind == "qk":
                                    qk_turn(i, j, 4 * i + j)
                                if kind == "mix":
                                    mix_turn(4 * i + j)

                        def qk_turn(i, j, s):
                            pe.wait_ge(sq_done.h, sq_done.at(s + 1))
                            pe.wait_ge(root_done.h, root_done.at(s))
                            pe.matmul(stat_ps[:, 0:T], ones[:], sq[:, 0:T], start=True, stop=True)
                            pe.matmul(stat_ps[:, T:W], ones[:], sq[:, T:W], start=True, stop=True).then_inc(sums_done.h, 1)
                            if not (first(i) and j == 0):
                                pe.wait_ge(qn_done.h, qn_done.at(s))
                                pe.wait_ge(rot_read.h, rot_read.at(s - 1))
                                pe.matmul(rot_ps, rot[:], qn[:, 0:T], start=True, stop=True).then_inc(rot_done.h, 1)

                        def mix_turn(c):
                            g = c // 2
                            if c == 0:
                                pe.wait_ge(mix_in.h, mix_in.at(64))
                            if c % 2 == 0:
                                pe.wait_ge(uf_in.h, uf_in.at(16 * (g + 1)))
                                if c == 0:
                                    pe.wait_ge(q_done.h, q_done.at(units))
                                    pe.wait_ge(root_done.h, root_done.at(units + 1))
                                pe.wait_ge(pool_out.h, pool_out.at(g))
                                pe.wait_ge(four_out.h, four_out.at(g))
                                for m in range(nch):
                                    dst = psum[2][:, m * 256:(m + 1) * 256] if m < 4 else bank(6)[:, (m - 4) * 256:(m - 3) * 256]
                                    ins = pe.matmul(dst, uf[:, m * P:(m + 1) * P], cs_fw[:, g * 256:(g + 1) * 256], start=True, stop=True)
                                ins.then_inc(chan_done.h, 1)
                            else:
                                pe.wait_ge(y_copied.h, y_copied.at(g + 1))
                                if both_w:
                                    for m in range(2):
                                        pe.matmul(f_ctx, y[:, 4 + m, 0:P], cn[:, m, 0:T:2], start=m == 0, stop=False)
                                        pe.matmul(f_ctx, y[:, 4 + m, P:2 * P], sn[:, m, 0:T:2], start=False, stop=m == 1)
                                for m in range(4):
                                    pe.matmul(f_lat, y[:, m, 0:P], cn[:, m, :], start=m == 0, stop=False)
                                    ins = pe.matmul(f_lat, y[:, m, P:2 * P], sn[:, m, :], start=False, stop=m == 3)
                                ins.then_inc(four_done.h, 1)
                                pe.wait_ge(pooled.h, pooled.at(g + 1))
                                for a, b in ((0, T), (T, W)) if both_w else ((0, T),):
                                    ins = pe.matmul(pool_ps[:, a:b], pw[:, g, :], pl[g][:, a:b], start=True, stop=True)
                                ins.then_inc(pool_done.h, 1)
                        turns(st, iters, body, kind)
            for r in raw_full:
                r.base += 16 * IN2 // 4
            for s in (hi_done, lo_done, w_used, staged):
                s.base += IN2
            for q in range(2):
                stored[q].base += 16 * IN2 // 2
            for q in range(4):
                q_in[q].base += 48
                q_out[q].base += 48 if q < 2 else 32
            for s, v in ((rope_in, 32), (mix_in, 64), (sq_done, 12), (sums_done, 12), (root_done, 11), (qn_done, 11),
                         (rot_done, 11), (rot_read, 10), (q_done, 10), (up_in, 64 * len(tok)), (uf_in, 64), (cnt_in, 64),
                         (pgate_in, 64), (fgate_in, 64), (pool_st, 64), (four_st, 64), (chan_done, 4), (y_copied, 4),
                         (four_done, 4), (pooled, 4), (pool_done, 4), (p_tanh, 4), (f_tanh, 4), (pool_out, 4), (four_out, 4)):
                s.base += v

        def final_norm():
            with nc.Block() as block:
                @block.tensor
                def _(pe):
                    pe.matmul(bank(0), ones[:], acc_sq[:, 0:T], start=True, stop=True).then_inc(m3.h, 1)

                @block.scalar
                def _(act):
                    act.wait_ge(m3.h, m3.at(1))
                    act.activation(tmp[:, 0:T], bank(0), ACT.Sqrt, bias=lam[:, 7:8], scale=1.0 / D).then_inc(m4.h, 1)

                @block.vector
                def _(dve):
                    st = Steps(dve, vv)
                    dve.wait_ge(m4.h, m4.at(1))
                    dve.reciprocal(rstd[:, 0:T], tmp[:, 0:T]).then_inc(st.step(), 1)
                    dve.wait_ge(st.sem, st.now)
                    for k in range(KC):
                        x = xk[:, k, 0:T]
                        dve.scalar_tensor_tensor(x, x, col("final", k), rstd[:, 0:T], ALU.mult, ALU.mult).then_inc(m1.h, 1)
                    st.end()

                @block.sync
                def _(sp):
                    for q in range(4):
                        sp.wait_ge(m1.h, m1.at(4 * q + 4))
                        sp.dma_start(out[:, 4 * q:4 * q + 4, :], xk[:, 4 * q:4 * q + 4, 0:T]).then_inc(m2.h, 16)
                    sp.wait_ge(m2.h, m2.at(64))

        setup()
        normalise([(0, T, lambda k: col("norm_pre", k), None), (T, W, lambda k: col("norm_mem", k), None)], False, load=load_x_mem)
        linear(2, lambda n: row(w_in, n), KC, 0, [(0, T)], store=lambda n: row(proj, n))
        ssm_prepare()
        for l in range(LAYERS):
            ssm_half(l)
            ada_finish(l)
        linear(2, lambda n: row(w_mem, n), KC, 0, [(T, W)], store=lambda n: row(mkv, n))
        glu()
        rope_tables()
        diff_attention()
        mem_units = [(b * P, 0, CT) for b in range(TB)]
        attention(4, 1, mem_units, CT, T, lambda h: row(proj, h + 32), lambda h: row(mkv, h), lambda h: row(mkv, h + 4),
                  lambda h: row(proj, h + 36), 12)
        out_projection(w_out, 0, [(0, T)], None)
        between_blocks()
        for l in range(LAYERS):
            last = l == LAYERS - 1
            normalise([(0, T, lambda k: mods[:, l, 16 + k, 0:1], lambda k: mods[:, l, k, 0:1]),
                       (T, W, lambda k: mods[:, l, 16 + k, 1:2], lambda k: mods[:, l, k, 1:2])], bool(l))
            both = [(0, T), (T, W)]
            projections(l)
            units = [(b * P, 0, W) for b in range(TB)]
            if not last:
                units[0:0] = [(T, T, CT)]
                units[5:5] = [(T + P, T, CT)]
            width = T if last else W

            def gate(h):
                return row(proj2, h + 28)[:, 0:width]

            def query(h):
                return row(proj2, h)[:, 0:width]
            attention(HEADS2, HEADS2 // KV2, units, W, width, query, lambda kv: proj2[8 + kv], lambda kv: proj2[10 + kv],
                      gate, 0, mixed=True)
            out_projection(w_out2, 16 * l, [(0, T)] if last else both, l)
        final_norm()


def _cols(a, n):
    return np.asarray(a, np.float32).reshape(n, P).T


def _blocks(w):
    k, n = w.shape
    return np.ascontiguousarray(w.reshape(k // P, P, n // P, P).transpose(2, 1, 0, 3).reshape(n // P, P, k))


def _feature_major(a):
    t, f = a.shape
    return np.ascontiguousarray(a.T.reshape(f // P, P, t).transpose(1, 0, 2))


def _constants():
    f = np.float32
    ident = np.eye(P, dtype=f)
    rot = np.zeros((P, P), f)
    for p in range(P):
        if p % 64 < 32:
            rot[p + 32, p] = -1.0
        else:
            rot[p - 32, p] = 1.0
    mask = np.where(np.arange(P)[None, :] <= np.arange(P)[:, None], 0.0, MASK).astype(f)
    inv = (f(10000.0) ** (-np.arange(0, 64, 2, dtype=f) / f(64))).astype(f)
    t = np.arange(T)
    p = np.arange(P)
    place = np.where(p[:, None] < 64, (t // 64)[None, :], (t % 64)[None, :]).astype(f)
    ang = (place * inv[p % 32][:, None]).astype(f).astype(np.float64)
    rope2 = np.concatenate([np.cos(ang), np.sin(ang)], 1).astype(f)
    n = np.arange(T)
    a = 2 * np.pi * ((n[:, None] * n[None, :]) % T) / T
    cn = np.cos(a).reshape(4, P, T).transpose(1, 0, 2).reshape(P, 4 * T)
    sn = np.sin(a).reshape(4, P, T).transpose(1, 0, 2).reshape(P, 4 * T)
    c = np.arange(P)
    b = 2 * np.pi * ((c[:, None] * c[None, :]) % P) / P
    cs = np.concatenate([np.cos(b), -np.sin(b)], 1).astype(f)
    cnt = np.zeros((4, W), f)
    for g in range(4):
        win = 2 << g
        for o, m in ((0, T), (T, CT)):
            q = np.arange(m)
            lo, hi = np.clip(q - win // 2, 0, m - 1), np.clip(q + win // 2 - 1, 0, m - 1)
            cnt[g, o:o + m] = 1.0 / (hi - lo + 1)
    return (np.concatenate([ident, rot, mask], 1), rope2, np.concatenate([cn, sn], 1).astype(f), cs, cnt,
            inv[p % 32][:, None])


def kernel(**inputs):
    import concourse.bacc as bacc
    from concourse.bass_utils import run_bass_kernel_spmd

    v = {k: np.asarray(a) for k, a in inputs.items()}
    const, rope2, cn_sn, cs, cnt, inv = _constants()

    def states(a):
        return a.reshape(SSM_TILES, P).T
    lamv = np.zeros((P, 4), np.float32)
    for q, name in enumerate(("diff_lq1", "diff_lq2", "diff_lk1", "diff_lk2")):
        lamv[0:64, q] = v[name][0]
    cond = np.stack([_cols(v["c_2"][0], KC), _cols(v["c_ctx_2"], KC)], 2).reshape(P, 32)
    parts = {
        "norm_pre": _cols(v["norm_pre"][0], 16), "norm_post": _cols(v["norm_post"][0], 16),
        "norm_mem": _cols(v["norm_mem"][0], 16),
        "norm_g": np.concatenate([_cols(v["norm_g_2"][l], 16) for l in range(2)], 1),
        "final": _cols(v["final_norm_g_2"], 16),
        "qk_gain": np.concatenate([np.concatenate([np.repeat(v["q_norm_g_2"][l][:, None], 8, 1),
                                                   np.repeat(v["k_norm_g_2"][l][:, None], 2, 1)], 1) for l in range(2)], 1),
        "pool_scale": np.concatenate([_cols(v["pool_scale_2"][l], 4) for l in range(2)], 1),
        "b_glu": _cols(v["b_glu"][0], 8), "ssm_d": _cols(v["ssm_d"][0].reshape(-1), 8),
        "subln": v["diff_subln"][0][:, None],
        "ada_b": np.concatenate([_cols(v["ada_b_2"][l], 48) for l in range(2)], 1),
        "cond": cond, "lam": lamv, "a_re": states(v["ssm_a_re"][0]), "a_im": states(v["ssm_a_im"][0]),
        "log_dt": states(np.repeat(v["ssm_log_dt"][0][:, None], 64, 1)), "inv_freq": inv,
    }
    cp = np.zeros((P, NCOL), np.float32)
    for name, a in parts.items():
        cp[:, COLS[name]:COLS[name] + a.shape[1]] = a
    bt = np.zeros((SSM_CH, P, 4, 2, P), np.float32)
    ct = np.zeros((P, SSM_TILES, 2, 32), np.float32)
    for g in range(64):
        c, j, s = g // 8, (g % 8) // 2, g % 2
        r = 32 * j + 16 * s
        for z, (bn, cn_) in enumerate((("ssm_b_re", "ssm_c_re"), ("ssm_b_im", "ssm_c_im"))):
            bt[c, r:r + 16, j, z, 64 * s:64 * s + 64] = v[bn][0, g].T
            ct[64 * s:64 * s + 64, g // 2, z, 16 * s:16 * s + 16] = v[cn_][0, g].T
    glu = _blocks(v["w_glu"][0]).reshape(4, 2, P, 1024).transpose(0, 2, 1, 3).reshape(4, P, D)
    order = np.r_[0:20, 28:36, 20:28]
    arrays = {
        "cp": cp, "const": const, "rope2": rope2, "cn_sn": cn_sn, "cs": cs, "invcnt": cnt,
        "pos": v["positions"].astype(np.int32).reshape(1, T),
        "x_in": _feature_major(v["x"][0]), "mem_in": _feature_major(v["mem"][0]), "ctx_in": _feature_major(v["ctx_2"][0]),
        "w_in": _blocks(v["w_in"][0]), "w_mem": _blocks(v["w_mem_kv"][0]), "w_glu": np.ascontiguousarray(glu),
        "w_out": _blocks(v["w_out"][0]),
        "w_in2": np.concatenate([_blocks(v["w_in_2"][l])[order] for l in range(2)]),
        "w_out2": np.concatenate([_blocks(v["w_out_2"][l]) for l in range(2)]),
        "ada_w": np.ascontiguousarray(v["ada_w_2"].reshape(2 * KC * P, 3 * D)),
        "ssm_b": bt.reshape(SSM_CH, P, 4 * 2 * P), "ssm_c": ct.reshape(P, SSM_TILES * 64),
        "pool_w": np.ascontiguousarray(v["pool_w_2"].transpose(0, 2, 1, 3)),
        "four_w": np.ascontiguousarray(v["fourier_w_2"].transpose(0, 2, 1, 3)),
    }
    nc = bacc.Bacc("TRN2", target_bir_lowering=False, num_devices=1, dynamic_dma_scratch_size=256)
    aps = {}
    for name, a in arrays.items():
        arrays[name] = a = np.ascontiguousarray(a)
        aps[name] = nc.dram_tensor(name, a.shape, mybir.dt.from_np(a.dtype), kind="ExternalInput").ap()
    ada = aps["ada_w"]

    class Slices:

        def __getitem__(self, key):
            l, r = key
            return lambda n: ada[bass.ds(n * P + l * D, P), r * D:(r + 1) * D] if not isinstance(n, int) else \
                ada[l * D + n * P:l * D + (n + 1) * P, r * D:(r + 1) * D]
    aps["ada_w"] = Slices()
    out = nc.dram_tensor("y_out_dram", (P, KC, T), F32, kind="ExternalOutput").ap()
    program(nc, out=out, **aps)
    r = run_bass_kernel_spmd(nc, [arrays], core_ids=[0])
    y = r.results[0]["y_out_dram"]
    return np.ascontiguousarray(y.transpose(1, 0, 2).reshape(D, T).T).reshape(1, T, D)
```
